# Optimizing a Trainium2 kernel written in Bass

```python
import jax, jax.numpy as jnp
from jax import lax
import numpy as np

D_MODEL = 1024
BATCH = 1
SEQ = 1024
DEPTH = 1

D_CONV = D_MODEL // 2
D_ATTN = D_MODEL - D_CONV
D_MIX = D_CONV + D_ATTN
HEAD_DIM = 64
N_HEADS = D_ATTN // HEAD_DIM
CONV_GROUPS = D_CONV // HEAD_DIM
CONV_WIDTH = 3
ROPE_DIM = HEAD_DIM // 4
ROPE_THETA = 500000.0
N_IDX_HEADS = 8
IDX_DIM = 64
TOPK_MAX = 256
Q_BLOCK = 128
EPS = 1e-6

kernel_name = "hybrid_conv_dsa_parallel_heads"

SPLIT_SIZES = [D_CONV, D_CONV, D_CONV, D_CONV,
               D_ATTN, D_ATTN, D_ATTN, D_ATTN,
               N_IDX_HEADS * IDX_DIM, IDX_DIM, N_IDX_HEADS]
D_IN = sum(SPLIT_SIZES)

def rmsnorm(x, gain):
    xf = x.astype(jnp.float32)
    inv = lax.rsqrt(jnp.mean(xf * xf, axis=-1, keepdims=True) + EPS)
    return (xf * inv).astype(x.dtype) * gain

def group_rmsnorm(y, gain, n_groups):
    shp = y.shape
    yg = y.reshape(shp[:-1] + (n_groups, shp[-1] // n_groups)).astype(jnp.float32)
    inv = lax.rsqrt(jnp.mean(yg * yg, axis=-1, keepdims=True) + EPS)
    return (yg * inv).reshape(shp).astype(y.dtype) * gain

def rope_partial(x, positions):
    half = ROPE_DIM // 2
    inv_freq = ROPE_THETA ** (-jnp.arange(half, dtype=jnp.float32) / half)
    ang = positions.astype(jnp.float32)[..., None] * inv_freq
    cos = jnp.cos(ang)[:, :, None, :]
    sin = jnp.sin(ang)[:, :, None, :]
    xr = x[..., :ROPE_DIM].astype(jnp.float32)
    x1, x2 = xr[..., :half], xr[..., half:]
    rot = jnp.concatenate([x1 * cos - x2 * sin, x1 * sin + x2 * cos], axis=-1).astype(x.dtype)
    return jnp.concatenate([rot, x[..., ROPE_DIM:]], axis=-1)

def short_conv_mixer(b_gate, c_gate, u, conv_w, conv_b):
    s = c_gate * u
    L = s.shape[1]
    sp = jnp.pad(s, ((0, 0), (CONV_WIDTH - 1, 0), (0, 0)))
    conv = conv_b + sum(conv_w[j] * sp[:, j:j + L, :] for j in range(CONV_WIDTH))
    return b_gate * conv

def dsa_sparse_attention(q, k, v, q_idx, k_idx, w_idx):
    Bsz, L = q.shape[0], q.shape[1]
    topk = min(TOPK_MAX, L // 4)
    n_blocks = L // Q_BLOCK
    idx_scale = IDX_DIM ** -0.5
    att_scale = HEAD_DIM ** -0.5
    key_pos = jnp.arange(L)
    gather = jax.vmap(lambda kb, ib: kb[ib])

    def block(i):
        t0 = i * Q_BLOCK
        q_b = lax.dynamic_slice_in_dim(q, t0, Q_BLOCK, axis=1)
        qi_b = lax.dynamic_slice_in_dim(q_idx, t0, Q_BLOCK, axis=1)
        wi_b = lax.dynamic_slice_in_dim(w_idx, t0, Q_BLOCK, axis=1)
        tq = t0 + jnp.arange(Q_BLOCK)
        dots = jnp.einsum('bqhd,bsd->bqhs', qi_b, k_idx) * idx_scale
        score = jnp.einsum('bqh,bqhs->bqs', wi_b.astype(jnp.float32),
                           jax.nn.relu(dots).astype(jnp.float32))
        causal = key_pos[None, :] <= tq[:, None]
        score = jnp.where(causal[None], score, -jnp.inf)
        _, sel = lax.top_k(score, topk)
        valid = sel <= tq[None, :, None]
        k_sel = gather(k, sel)
        v_sel = gather(v, sel)
        logits = jnp.einsum('bqhd,bqkhd->bqhk', q_b, k_sel).astype(jnp.float32) * att_scale
        logits = jnp.where(valid[:, :, None, :], logits, -jnp.inf)
        p = jax.nn.softmax(logits, axis=-1).astype(v.dtype)
        return jnp.einsum('bqhk,bqkhd->bqhd', p, v_sel)

    outs = lax.map(block, jnp.arange(n_blocks))
    return jnp.transpose(outs, (1, 0, 2, 3, 4)).reshape(Bsz, L, N_HEADS * HEAD_DIM)

def hybrid_layer(x, c, positions, w_ada, b_ada, norm_in, w_in, conv_w, conv_b,
                 gn_conv, gn_attn, w_out):
    Bsz, L, _ = x.shape
    mod = jax.nn.silu(c) @ w_ada + b_ada
    shift, scale, gate = jnp.split(mod, 3, axis=-1)
    h = rmsnorm(x, norm_in) * (1.0 + scale[:, None, :]) + shift[:, None, :]

    proj = h @ w_in
    cuts = [int(v) for v in np.cumsum(SPLIT_SIZES)[:-1]]
    (cb, cc, cu, cz, aq, ak, av, az, iq, ik, iw) = jnp.split(proj, cuts, axis=-1)

    y_conv = short_conv_mixer(cb, cc, cu, conv_w, conv_b)
    y_conv = group_rmsnorm(y_conv, gn_conv, CONV_GROUPS) * jax.nn.silu(cz)

    q = rope_partial(aq.reshape(Bsz, L, N_HEADS, HEAD_DIM), positions)
    k = rope_partial(ak.reshape(Bsz, L, N_HEADS, HEAD_DIM), positions)
    v = av.reshape(Bsz, L, N_HEADS, HEAD_DIM)
    q_idx = rope_partial(iq.reshape(Bsz, L, N_IDX_HEADS, IDX_DIM), positions)
    k_idx = rope_partial(ik[:, :, None, :], positions)[:, :, 0, :]
    w_idx = iw * (N_IDX_HEADS ** -0.5)
    y_attn = dsa_sparse_attention(q, k, v, q_idx, k_idx, w_idx)
    y_attn = group_rmsnorm(y_attn, gn_attn, N_HEADS) * jax.nn.silu(az)

    y = jnp.concatenate([y_conv, y_attn], axis=-1) @ w_out
    return x + gate[:, None, :] * y

def setup_inputs(seed: int = 0) -> dict:
    key = jax.random.key(seed)
    ks = jax.random.split(key, 14)
    f32 = jnp.float32
    x = jax.random.normal(ks[0], (BATCH, SEQ, D_MODEL), f32)
    c = jax.random.normal(ks[1], (BATCH, D_MODEL), f32)
    offsets = jax.random.randint(ks[2], (BATCH, 1), 0, 1024, dtype=jnp.int32)
    positions = (jnp.arange(SEQ, dtype=jnp.int32)[None, :] + offsets).astype(jnp.int32)
    w_ada = jax.random.normal(ks[3], (D_MODEL, 3 * D_MODEL), f32) * (0.5 * D_MODEL ** -0.5)
    b_ada = jax.random.normal(ks[4], (3 * D_MODEL,), f32) * 0.1
    norm_in = 1.0 + 0.05 * jax.random.normal(ks[5], (D_MODEL,), f32)
    w_in = jax.random.normal(ks[6], (D_MODEL, D_IN), f32) * (D_MODEL ** -0.5)
    conv_w = jax.random.normal(ks[7], (CONV_WIDTH, D_CONV), f32) * (CONV_WIDTH ** -0.5)
    conv_b = jax.random.normal(ks[8], (D_CONV,), f32) * 0.02
    gn_conv = 1.0 + 0.05 * jax.random.normal(ks[9], (D_CONV,), f32)
    gn_attn = 1.0 + 0.05 * jax.random.normal(ks[10], (D_ATTN,), f32)
    w_out = jax.random.normal(ks[11], (D_MIX, D_MODEL), f32) * (D_MIX ** -0.5)
    norm_f = 1.0 + 0.05 * jax.random.normal(ks[12], (D_MODEL,), f32)
    return {"x": x, "c": c, "positions": positions, "w_ada": w_ada, "b_ada": b_ada,
            "norm_in": norm_in, "w_in": w_in, "conv_w": conv_w, "conv_b": conv_b,
            "gn_conv": gn_conv, "gn_attn": gn_attn, "w_out": w_out, "norm_f": norm_f}

def reference(x, c, positions, w_ada, b_ada, norm_in, w_in, conv_w, conv_b,
              gn_conv, gn_attn, w_out, norm_f):
    h = x
    for _ in range(DEPTH):
        h = hybrid_layer(h, c, positions, w_ada, b_ada, norm_in, w_in, conv_w, conv_b,
                         gn_conv, gn_attn, w_out)
    return rmsnorm(h, norm_f)


_drawn_inputs = setup_inputs


def setup_inputs(seed=0):
    import zlib

    import numpy as np

    out = dict(_drawn_inputs(seed))
    spreads = {}
    factors = {'conv_b': 8.0, 'gn_conv': 7.071, 'gn_attn': 7.071}
    for name, (base, spread) in spreads.items():
        noise = np.random.default_rng([zlib.crc32(name.encode()), seed]).standard_normal(out[name].shape)
        drawn = base * np.exp(spread * noise) if base else spread * noise
        out[name] = __import__('jax').numpy.asarray(drawn.astype(out[name].dtype))
    for name, factor in factors.items():
        out[name] = (out[name] * factor).astype(out[name].dtype)
    return out
```

```python
from contextlib import ExitStack

import numpy as np

import concourse.bass as bass
from concourse import mybir

P = 128
D = 1024
S = 1024
KT = D // P
NB = S // P
HD = 64
NH = 8
NIH = 8
NT = 4
ROPE = 16
TOPK = 256
ROUND = 8
HALF = 512
EPS = 1e-6
IDX_SCALE = float(HD) ** -0.5 * float(NIH) ** -0.5
ATT_SCALE = float(HD) ** -0.5
TAKEN = -3.0e38
FUTURE = -3.3e38
BIG = 1.0e30
MAGIC = 1.5 * 2.0 ** 23
PI = 3.1415925

F32 = mybir.dt.float32
F32R = mybir.dt.float32r
BF16 = mybir.dt.bfloat16
I32 = mybir.dt.int32
ALU = mybir.AluOpType
ACT = mybir.ActivationFunctionType

V_C, V_NORM, V_BSH, V_BSC = 0, 8, 16, 24
V_CW, V_CB, V_GC, V_GA = 32, 44, 48, 52
V_FREQ, V_SIGN, V_EPS, V_COLS = 56, 57, 58, 64


def two_pi_parts():
    left, parts = 2 * np.pi, []
    for _ in range(3):
        m, e = np.frexp(left)
        parts.append(float(np.round(m * 256) / 256 * 2.0 ** e))
        left -= parts[-1]
    return parts + [float(left)]


UNITS = ([("ik", 0)] + [("iq", t) for t in range(NT)] + [("aq", t) for t in range(NT)]
         + [("ak", t) for t in range(NT)] + [("av", t) for t in range(NT)]
         + [(s, t) for t in range(NT) for s in ("cc", "cu", "cb", "cz")] + [("az", t) for t in range(NT)])
NU = len(UNITS)
UNIT = {u: n for n, u in enumerate(UNITS)}
STARTS = {s: 512 * i for i, s in enumerate(("cb", "cc", "cu", "cz", "aq", "ak", "av", "az", "iq"))}
NRAW = 3


def schedule():
    after = {
        ("iq", 0): [("iwt", 0)],
        ("aq", 0): [("idx", 2), ("idx", 3)],
        ("aq", 1): [("idx", 4), ("idx", 5)],
        ("aq", 2): [("idx", 6)],
        ("aq", 3): [("idx", 7)],
        ("av", 1): [("vt", 0)],
        ("av", 2): [("vt", 1)],
        ("av", 3): [("vt", 2)],
        ("cc", 0): [("vt", 3)],
    }
    for t in range(NT):
        n = UNIT[("cz", t)] + 1
        after.setdefault(UNITS[n], []).append(("cn", t))
    out = []
    for n, u in enumerate(UNITS):
        out.append(("unit", n))
        out += after.get(u, [])
    return out


SCHEDULE = schedule()
SPLITS = {("unit", UNIT[("iq", 3)]): "iq", ("idx", NB - 1): "aq", ("unit", UNIT[("cc", 0)]): "ak"}
IDX_BLOCKS = range(TOPK // P, NB)
SUMS_AFTER = {2: 0, 4: 1, 6: 2, 7: 3}


def build(nc, a):
    with ExitStack() as ctx:
        base = 16512
        used = [0]

        def at(name, shape, dt, kb):
            off = base + int(kb * 1024)
            assert off % 32 == 0
            return nc.alloc_sbuf_tensor_at(name, shape, dt, offset=off)

        def sem(name):
            return ctx.enter_context(nc.semaphore(name))

        arena = ctx.enter_context(nc.sbuf_tensor("arena", [P, 207 * 256], F32))

        hH = at("hH", [P, KT, S], F32R, 0)
        hL = at("hL", [P, KT, S], F32R, 32)
        raw = at("raw", [P, NRAW, KT, P], F32, 64)
        wH = at("wH", [P, 2, KT, P], F32R, 76)
        wL = at("wL", [P, 2, KT, P], F32R, 84)
        bias = at("bias", [P, 36 * P], BF16, 92)
        score = at("score", [P, 33 * P], F32, 93.5)
        identF = at("identF", [P, P], F32, 110)
        pairs = at("pairs", [P, P], F32, 110.5)
        identB = at("identB", [P, P], BF16, 111)
        onesB = at("onesB", [16, P], BF16, 111.25)
        vec = at("vec", [P, V_COLS], F32, 111.5)
        wabs = at("wabs", [P, NB, NIH], F32, 111.75)
        wsgn = at("wsgn", [P, NB, NIH], F32, 112)
        small = at("small", [P, 64], F32, 112.25)
        onesF = at("onesF", [P, 1], F32, 112.5)
        m8 = at("m8", [P, ROUND], F32, 112.5625)
        mx = at("mx", [P, NB], F32, 112.625)
        mparts = at("mparts", [P, 2 * NB], BF16, 112.6875)
        csilu = small[:, 0:8]
        sumsq = small[:, 8:16]
        rstd = small[:, 16:24]
        shift = small[:, 24:32]
        amp = small[:, 32:40]
        fin = small[:, 40:48]
        finr = small[:, 48:56]
        xin = at("xin", [P, NB, D], F32, 113)
        xT = at("xT", [P, KT, S], F32, 145)
        wa = [at(f"wa{i}", [P, 2 * D], F32, kb) for i, kb in enumerate((177, 185, 93, 101))]
        acc = at("acc", [P, 2 * D], F32, 193)
        iqs = at("iqs", [P, NIH, S], F32R, 113)
        iks1 = at("iks1", [P, S], F32R, 145)
        iks2 = at("iks2", [P, S], F32R, 149)
        T = at("T", [P, NT, S], F32, 153)
        cx = at("cx", [P, S], F32, 169)
        cs = at("cs", [P, S], F32, 173)
        tabC = at("tabC", [P, S], F32, 177)
        tabS = at("tabS", [P, S], F32, 181)
        Tik = at("Tik", [P, S], F32, 185)
        hl = [at(f"hl{i}", [P, 2, S], F32R, 189 + 8 * i) for i in range(2)]
        relu = at("relu", [P, 2, S], F32, 197)
        posi = at("posi", [P, S], I32, 169)
        ang = at("ang", [P, S], F32, 173)
        turns = at("turns", [P, S], F32, 189)
        V = at("V", [P, NB, NT, 3 * HD], F32, 113)
        vst = at("vst", [P, 2, S], F32, 137)
        convc = at("convc", [P, S], F32, 145)
        convu = at("convu", [P, S], F32, 149)
        convs = at("convs", [P, 2 + S], F32, 153)
        conv0 = at("conv0", [P, S], F32, 157.25)
        conv1 = at("conv1", [P, S], F32, 161.5)
        convb = at("convb", [P, S], F32, 165.5)
        azs = at("azs", [P, NT, S], F32, 170)
        yconv = at("yconv", [P, NT, S], F32, 189)
        qs = [at(f"qs{i}", [P, S], F32R, 145 + 12 * i) for i in range(2)]
        ks1 = [at(f"ks1_{i}", [P, S], F32R, 149 + 12 * i) for i in range(2)]
        ks2 = [at(f"ks2_{i}", [P, S], F32R, 153 + 12 * i) for i in range(2)]
        prob = at("prob", [P, 4, HALF], F32, 137)
        mrow = at("mrow", [16, NB, P], BF16, 186)
        delta = at("delta", [16, NB, P], BF16, 205)
        ya = at("ya", [P, NT, S], F32, 64)
        rden = at("rden", [P, HALF], F32, 102)
        ysq = at("ysq", [P, S], F32, 104)
        onesq = at("onesq", [P, P], F32, 108)
        gw = at("gw", [P, 2, D], F32, 80)
        gate = at("gate", [P, D], F32, 88)
        yH = [at(f"yH{i}", [P, KT, P], F32R, 145 + 8 * i) for i in range(2)]
        yL = [at(f"yL{i}", [P, KT, P], F32R, 149 + 8 * i) for i in range(2)]
        normf = at("normf", [P, D], F32, 161)
        bgate = at("bgate", [P, D], F32, 165)
        xe = at("xe", [P, 2, D], F32, 113)
        oe = at("oe", [P, 2, D], F32, 121)
        te = at("te", [P, 2, D], F32, 129)

        ps = ctx.enter_context(nc.psum_tensor("ps", [P, 8, HALF], F32))

        def two(b):
            return ps[:, b:b + 2, :].rearrange("p b n -> p (b n)")

        dx = nc.dram_tensor("rope_x", [3, NH, ROPE, S], F32).ap()
        dp = nc.dram_tensor("rope_partner", [3, NH, ROPE, S], F32).ap()
        dr = nc.dram_tensor("rope_rotated", [3, NH, ROPE, S], F32).ap()
        dqk = nc.dram_tensor("qk_halves", [2, 2, NT, P, S], F32).ap()

        s_const = sem("s_const"); s_pos = sem("s_pos")
        s_x = [sem(f"s_x{t}") for t in range(NB)]
        s_wa = [sem(f"s_wa{i}") for i in range(4)]
        s_ones = sem("s_ones"); s_csilu = sem("s_csilu"); s_sumsq = sem("s_sumsq")
        s_var = sem("s_var"); s_std = sem("s_std"); s_xn = sem("s_xn")
        s_xtp = sem("s_xtp"); s_xt = sem("s_xt")
        s_acc = sem("s_acc"); s_modp = sem("s_modp")
        s_h = sem("s_h"); s_hH = sem("s_hH"); s_hL = sem("s_hL")
        s_red = sem("s_red"); s_trig = sem("s_trig"); s_tab = sem("s_tab")
        s_raw = [sem(f"s_raw{i}") for i in range(NRAW)]
        s_wH = sem("s_wH"); s_wL = sem("s_wL")
        s_unit = sem("s_unit"); s_evac = sem("s_evac")
        s_iwt = sem("s_iwt"); s_iw = sem("s_iw")
        s_cx = sem("s_cx"); s_rot = sem("s_rot"); s_back = sem("s_back"); s_bounce = sem("s_bounce")
        s_kiH = sem("s_kiH"); s_kiL = sem("s_kiL"); s_kidup = sem("s_kidup")
        s_splH = sem("s_splH"); s_splL = sem("s_splL")
        s_spill = [sem("s_spill0"), sem("s_spill1")]
        s_idx = sem("s_idx"); s_relu = sem("s_relu"); s_score = sem("s_score")
        s_caus = sem("s_caus"); s_round = sem("s_round"); s_mask = sem("s_mask")
        s_vt = sem("s_vt"); s_v = sem("s_v"); s_vones = sem("s_vones")
        s_cvs = sem("s_cvs"); s_cvt = sem("s_cvt"); s_cvy = sem("s_cvy"); s_cvq = sem("s_cvq")
        s_cvp = sem("s_cvp"); s_cvd = sem("s_cvd"); s_cvr = sem("s_cvr"); s_cvn = sem("s_cvn")
        s_pad = sem("s_pad"); s_onesq = sem("s_onesq")
        s_woH = sem("s_woH"); s_woLp = sem("s_woLp"); s_woLd = sem("s_woLd")
        s_stack = [sem("s_stack0"), sem("s_stack1")]
        s_delta = sem("s_delta")
        s_lg = sem("s_lg"); s_mx = sem("s_mx"); s_mp = sem("s_mp"); s_mt = sem("s_mt"); s_mrow = sem("s_mrow")
        s_st = sem("s_st"); s_exp = sem("s_exp"); s_pv = sem("s_pv"); s_o = sem("s_o")
        s_ysq = sem("s_ysq"); s_yss = sem("s_yss"); s_yln = sem("s_yln"); s_yrs = sem("s_yrs")
        s_yn = sem("s_yn"); s_ya = sem("s_ya")
        s_gw = [sem("s_gw0"), sem("s_gw1")]
        s_gacc = sem("s_gacc"); s_gp = sem("s_gp"); s_gate = sem("s_gate"); s_nf = sem("s_nf")
        s_yH = sem("s_yH"); s_yL = sem("s_yL"); s_op = sem("s_op"); s_og = sem("s_og")
        s_xe = [sem("s_xe0"), sem("s_xe1")]
        s_res = sem("s_res"); s_fsq = sem("s_fsq"); s_fv = sem("s_fv"); s_fs = sem("s_fs")
        s_fin = sem("s_fin")
        s_out = [sem("s_out0"), sem("s_out1")]
        own_act = sem("own_act"); own_dve = sem("own_dve"); own_pool = sem("own_pool")

        SECT = {"iq": 0, "aq": 1, "ak": 2}
        NBOUNCE = 6

        def score_of(i):
            o = (i * (i + 1) // 2 - 3) * P
            return score[:, o:o + (i + 1) * P]

        def bias_of(i):
            o = (i * (i + 1) // 2) * P
            return bias[:, o:o + (i + 1) * P]

        def rows(h):
            return slice(HD * (h % 2), HD * (h % 2) + HD)

        def chunks(sb):
            return [(j, max(0, j - 4 * sb)) for j in range(4 * sb + 4)]

        MAXIMA, SUMS = -1, -2
        ST = []
        for h in range(NH):
            ST.append((h, MAXIMA, 0, 0))
            for sb in range(2):
                ST += [(h, sb, j, c) for j, c in chunks(sb)]
            if h in SUMS_AFTER:
                ST += [(SUMS_AFTER[h], SUMS, half, 0) for half in range(2)]
        ST_AT = {u[:3]: n for n, u in enumerate(ST)}
        PV = [u for u in ST if u[1] >= 0]
        PV_AT = {u[:3]: n for n, u in enumerate(PV)}

        def section_low(engine, waits, sec, t):
            m = NT * SECT[sec] + t
            waits.wait_ge(s_splH, m + 1)
            engine.tensor_tensor(hl[m % 2][:, 1, :], T[:, t, :], hl[m % 2][:, 0, :].bitcast(F32),
                                 ALU.subtract).then_inc(s_splL, 1)

        def out_low(engine, waits, c, done):
            waits.wait_ge(s_woH, c + 1)
            engine.tensor_tensor(hL[:, c, :], raw[:, (NU + c) % NRAW, :, :].rearrange("p k n -> p (k n)"),
                                 hH[:, c, :].bitcast(F32), ALU.subtract).then_inc(done, 1)

        block = ctx.enter_context(nc.Block())

        @block.sync
        def _(sp):
            sp.dma_start(vec[:], a["vecs"]).then_inc(s_const, 16)
            sp.dma_start(identF[:], a["ident_f"]).then_inc(s_const, 16)
            sp.dma_start(pairs[:], a["pairs"]).then_inc(s_const, 16)
            sp.dma_start(identB[:], a["ident_b"]).then_inc(s_const, 16)
            for t in range(NB):
                sp.dma_start(xin[:, t, :], a["x"][0, P * t:P * t + P, :]).then_inc(s_x[t], 16)
            w_ada = a["w_ada"].rearrange("(k p) n -> k p n", p=P)
            for kt in range(KT):
                if kt >= 4:
                    sp.wait_ge(s_acc, kt - 3)
                sp.dma_start(wa[kt % 4][:], w_ada[kt, :, 0:2 * D]).then_inc(s_wa[kt % 4], 16)

            def load(n):
                if NRAW <= n < NU + NRAW:
                    sp.wait_ge(s_wL, n - NRAW + 1)
                elif n >= NU + NRAW:
                    c = n - NRAW - NU
                    sp.wait_ge(s_woH, c + 1)
                    sp.wait_ge((s_woLp, s_woLd)[c % 2], c // 2 + 1)
                if n == 0:
                    sp.dma_start(raw[:, 0, :, 0:72], a["w_ik"]).then_inc(s_raw[0], 16)
                elif n < NU:
                    sp.dma_start(raw[:, n % NRAW, :, :], a["w_units"][n - 1]).then_inc(s_raw[n % NRAW], 16)
                else:
                    sp.dma_start(raw[:, n % NRAW, :, :],
                                 a["w_out"][P * (n - NU):P * (n - NU) + P, :]
                                 .rearrange("p (k n) -> p k n", k=KT)).then_inc(s_raw[n % NRAW], 16)

            for n in range(NRAW):
                load(n)
            sp.wait_ge(s_hL, KT)
            sp.dma_start(posi[:], a["positions"][0:1, :].broadcast_to([P, S])).then_inc(s_pos, 16)

            def rope_out(sec):
                sp.wait_ge(s_evac, UNIT[(sec, NT - 1)] + 1)
                k = SECT[sec]
                for odd in range(2):
                    b = HD * odd
                    for (lo, n, dst, to) in ((0, 16, dx, 0), (0, 8, dp, 8), (8, 8, dp, 0)):
                        sp.dma_start(dst[k, odd::2, to:to + n, :].rearrange("t r s -> r t s"),
                                     T[b + lo:b + lo + n, :, :]).then_inc(s_bounce, 16)
                sp.wait_ge(s_bounce, 16 * NBOUNCE * (k + 1) + 32 * k)
                sp.wait_ge(s_back, 16 if k == 0 else 16 + 32 * k)
                sp.dma_start(cx[:], dx[k].rearrange("h r s -> (h r) s")).then_inc(s_cx, 16)
                sp.dma_start(cs[:], dp[k].rearrange("h r s -> (h r) s")).then_inc(s_cx, 16)

            def rope_back(sec):
                k = SECT[sec]
                sp.wait_ge(s_rot, k + 2)
                sp.dma_start(dr[k].rearrange("h r s -> (h r) s"), cx[:]).then_inc(s_bounce, 32)
                sp.wait_ge(s_bounce, (16 * NBOUNCE + 32) * (k + 1))
                for odd in range(2):
                    sp.dma_start(T[HD * odd:HD * odd + ROPE, :, :],
                                 dr[k, odd::2, :, :].rearrange("t r s -> r t s")).then_inc(s_back, 16)

            def spill(sec):
                for t in range(NT):
                    m = NT * SECT[sec] + t
                    sp.wait_ge(s_splH, m + 1)
                    sp.wait_ge(s_splL, m + 1)
                    for half in range(2):
                        if sec == "iq":
                            for odd in range(2):
                                sp.dma_start(iqs[HD * half:HD * half + HD, 2 * t + odd, :].bitcast(F32),
                                             hl[m % 2][HD * odd:HD * odd + HD, half, :].bitcast(F32)).then_inc(s_spill[m % 2], 16)
                        else:
                            sp.dma_start(dqk[SECT[sec] - 1, half, t], hl[m % 2][:, half, :].bitcast(F32)).then_inc(s_spill[m % 2], 32)

            for kind, n in SCHEDULE:
                if kind != "unit":
                    continue
                load(n + NRAW)
                if UNITS[n] == ("iq", 0):
                    sp.wait_ge(s_evac, 1)
                    sp.wait_ge(s_tab, 1)
                    sp.dma_start(cx[0:16, :], Tik[0:16, :]).then_inc(s_cx, 16)
                    sp.dma_start(cs[0:8, :], Tik[8:16, :]).then_inc(s_cx, 16)
                    sp.dma_start(cs[8:16, :], Tik[0:8, :]).then_inc(s_cx, 16)
                    sp.wait_ge(s_rot, 1)
                    sp.dma_start(Tik[0:16, :], cx[0:16, :]).then_inc(s_back, 16)
                if UNITS[n] == ("iq", 2):
                    sp.wait_ge(s_kiH, 1)
                    sp.dma_start(iks1[HD:P, :].bitcast(F32), iks1[0:HD, :].bitcast(F32)).then_inc(s_kidup, 16)
                    sp.wait_ge(s_kiL, 1)
                    sp.dma_start(iks2[HD:P, :].bitcast(F32), iks2[0:HD, :].bitcast(F32)).then_inc(s_kidup, 16)
                if UNITS[n] == ("iq", 3):
                    rope_out("iq")
                    rope_back("iq")
                    spill("iq")
                if UNITS[n] == ("aq", 3):
                    rope_out("aq")
                if UNITS[n] == ("ak", 0):
                    rope_back("aq")
                    spill("aq")
                if UNITS[n] == ("ak", 3):
                    rope_out("ak")
                if UNITS[n] == ("av", 3):
                    rope_back("ak")
                    spill("ak")

            sp.wait_ge(s_cvn, NT)
            sp.dma_start(delta[:], a["delta"]).then_inc(s_delta, 16)
            for i in range(2):
                sp.wait_ge(s_spill[i], 16 * (4 * 2 + 4 * 4))
            for h in range(NH):
                if h >= 2:
                    sp.wait_ge(s_st, ST_AT[(h - 2, 1, NB - 1)] + 1)
                t, r = h // 2, rows(h)
                for i, dst in enumerate((qs, ks1, ks2)):
                    for half in range(2):
                        part = half if i == 0 else i - 1
                        sp.dma_start(dst[h % 2][HD * half:HD * half + HD, :].bitcast(F32),
                                     dqk[min(i, 1), part, t, r, :]).then_inc(s_stack[h % 2], 16)
                if h == 1:
                    for n in range(NU + NRAW, NU + KT):
                        load(n)
                    sp.wait_ge(s_woLp, KT // 2)
                    sp.wait_ge(s_woLd, KT // 2)
                    sp.wait_ge(s_woH, KT)
                if 1 <= h <= 4:
                    for kt in (2 * h - 2, 2 * h - 1):
                        if kt >= 2:
                            sp.wait_ge(s_gacc, kt - 1)
                        sp.dma_start(gw[:, kt % 2, :], w_ada[kt, :, 2 * D:3 * D]).then_inc(s_gw[kt % 2], 16)

            sp.wait_ge(s_pv, len(PV))
            sp.dma_start(normf[:], a["norm_f"].rearrange("(o n) -> o n", o=1).broadcast_to([P, D])).then_inc(s_nf, 16)
            sp.dma_start(bgate[:], a["b_gate"].rearrange("(o n) -> o n", o=1).broadcast_to([P, D])).then_inc(s_nf, 16)
            for b in range(2):
                sp.dma_start(xe[:, b, :], a["x"][0, P * b:P * b + P, :]).then_inc(s_xe[b], 16)
            for b in range(NB):
                sp.wait_ge(s_fin, b + 1)
                sp.dma_start(a["out"][0, P * b:P * b + P, :], oe[:, b % 2, :]).then_inc(s_out[b % 2], 16)
                if b + 2 < NB:
                    sp.wait_ge(s_res, b + 1)
                    sp.dma_start(xe[:, b % 2, :], a["x"][0, P * (b + 2):P * (b + 3), :]).then_inc(s_xe[b % 2], 16)
            for i in range(2):
                sp.wait_ge(s_out[i], 16 * (NB // 2))

        @block.tensor
        def _(pe):
            pe.wait_ge(s_const, 16 * 4)
            for kt in range(KT):
                if kt == 0:
                    pe.wait_ge(s_xn, NB)
                if kt >= 4:
                    pe.wait_ge(s_xt, kt - 3)
                for t in range(NB):
                    mm = pe.transpose(two(2 * (kt % 4))[:, P * t:P * t + P], xin[:, t, P * kt:P * kt + P], identF[:])
                mm.then_inc(s_xtp, 1)
            pe.wait_ge(s_acc, KT)
            pe.wait_ge(s_ones, 1)
            pe.wait_ge(s_xt, KT)
            for j in range(2 * KT):
                mm = pe.matmul(ps[:, 0, j:j + 1], acc[:, P * j:P * j + P], onesF[:], start=(j == 0), stop=True,
                               skip_group_check=True)
            mm.then_inc(s_modp, 1)

            def unit(n):
                m = 72 if n == 0 else P
                pe.wait_ge(s_wH, n + 1)
                pe.wait_ge(s_wL, n + 1)
                if n >= 2:
                    pe.wait_ge(s_evac, n - 1)
                if n == 0:
                    pe.wait_ge(s_h, KT)
                for half in range(2):
                    out = ps[0:m, 2 * (n % 2) + half, :]
                    cols = slice(HALF * half, HALF * half + HALF)
                    for kt in range(KT):
                        if n == 0 and half == 0:
                            pe.wait_ge(s_hH, kt + 1)
                            pe.wait_ge(s_hL, kt + 1)
                        pe.matmul(out, wH[:, n % 2, kt, 0:m], hH[:, kt, cols], start=(kt == 0), stop=False)
                        pe.matmul(out, wH[:, n % 2, kt, 0:m], hL[:, kt, cols], start=False, stop=False)
                        mm = pe.matmul(out, wL[:, n % 2, kt, 0:m], hH[:, kt, cols], start=False, stop=(kt == KT - 1))
                mm.then_inc(s_unit, 1)

            def index_scores(i):
                n = (i + 1) * P
                for h in range(NIH):
                    u = NIH * (i - 2) + h
                    if u == 0:
                        pe.wait_ge(s_kidup, 32)
                        pe.wait_ge(s_spill[0], 16 * 8)
                        pe.wait_ge(s_spill[1], 16 * 8)
                        pe.wait_ge(s_iw, 1)
                    if u >= 2:
                        pe.wait_ge(s_relu, u - 1)
                    dst = two(4 + 2 * (u % 2))
                    for o in range(0, n, HALF):
                        e = min(n, o + HALF)
                        pe.matmul(dst[:, o:e], iqs[:, h, P * i:P * i + P], iks1[:, o:e], start=True, stop=False)
                        mm = pe.matmul(dst[:, o:e], iqs[:, h, P * i:P * i + P], iks2[:, o:e], start=False, stop=True)
                    mm.then_inc(s_idx, 1)

            for kind, n in SCHEDULE:
                if kind == "unit":
                    unit(n)
                elif kind == "iwt":
                    pe.wait_ge(s_evac, 1)
                    for b in range(NB):
                        mm = pe.transpose(ps[:, 4, NIH * b:NIH * b + NIH], Tik[64:72, P * b:P * b + P], identF[64:72, 64:72])
                    mm.then_inc(s_iwt, 1)
                elif kind == "idx":
                    index_scores(n)
                elif kind == "vt":
                    pe.wait_ge(s_evac, UNIT[("av", n)] + 1)
                    if n == 0:
                        pe.wait_ge(s_relu, 8 * len(IDX_BLOCKS))
                    if n >= 2:
                        pe.wait_ge(s_v, n - 1)
                    for b in range(NB):
                        mm = pe.transpose(two(4 + 2 * (n % 2))[:, P * b:P * b + P], vst[:, n % 2, P * b:P * b + P], identF[:])
                    mm.then_inc(s_vt, 1)
                elif kind == "cn":
                    pe.wait_ge(s_cvq, n + 1)
                    if n == 0:
                        pe.wait_ge(s_v, NT)
                    else:
                        pe.wait_ge(s_cvd, n)
                    for half in range(2):
                        mm = pe.matmul(ps[:, 4 + half, :], pairs[:], conv0[:, HALF * half:HALF * half + HALF], start=True, stop=True)
                    mm.then_inc(s_cvp, 1)

            def logits(h):
                pe.wait_ge(s_stack[h % 2], 96 * (h // 2 + 1))
                for i in range(NB):
                    u = NB * h + i
                    n = (i + 1) * P
                    if u == 0:
                        pe.wait_ge(s_evac, NU)
                    if u >= 2:
                        pe.wait_ge(s_mx, u - 1)
                    dst = two(2 * (u % 2))
                    for o in range(0, n, HALF):
                        e = min(n, o + HALF)
                        pe.matmul(dst[:, o:e], qs[h % 2][:, P * i:P * i + P], ks1[h % 2][:, o:e], start=True, stop=False)
                        mm = pe.matmul(dst[:, o:e], qs[h % 2][:, P * i:P * i + P], ks2[h % 2][:, o:e], start=False, stop=True)
                    mm.then_inc(s_lg, 1)

            def st_slot(u):
                if u == 0:
                    pe.wait_ge(s_cvd, NT)
                if u >= 2:
                    hh, sb, j, _ = ST[u - 2]
                    if sb == MAXIMA:
                        pe.wait_ge(s_mrow, hh + 1)
                    elif sb == SUMS:
                        pe.wait_ge(s_yln, 2 * hh + j + 1)
                    else:
                        pe.wait_ge(s_exp, PV_AT[(hh, sb, j)] + 1)
                return 4 + u % 2

            def maxima(h):
                bank = st_slot(ST_AT[(h, -1, 0)])
                pe.wait_ge(s_mp, h + 1)
                pe.transpose(ps[0:16, bank, :].bitcast(BF16)[:, 0:P], mparts[:], identB[:]).then_inc(s_mt, 1)

            def scores_t(u):
                h, sb, j, c = ST[u]
                if (sb, j) == (0, 0):
                    pe.wait_ge(s_mrow, h + 1)
                bank = st_slot(u)
                out = ps[:, bank, P * c:HALF]
                cols = slice(HALF * sb + P * c, HALF * sb + HALF)
                keys = slice(P * j, P * j + P)
                pe.matmul(out, ks1[h % 2][:, keys], qs[h % 2][:, cols], start=True, stop=False, skip_group_check=True)
                pe.matmul(out, ks2[h % 2][:, keys], qs[h % 2][:, cols], start=False, stop=False, skip_group_check=True)
                for b in range(c, 4):
                    i = 4 * sb + b
                    if i >= 2 or i == j:
                        pe.matmul(ps[:, bank, P * b:P * b + P], bias_of(i)[:, keys], identB[:], start=False, stop=False,
                                  skip_group_check=True)
                pe.matmul(out, onesB[:], mrow[:, 4 * sb + c:4 * sb + 4, :].rearrange("p b n -> p (b n)"), start=False,
                          stop=True, skip_group_check=True).then_inc(s_st, 1)

            def values(k):
                h, sb, j, c = PV[k]
                pe.wait_ge(s_exp, k + 1)
                if j == 0 and 2 * h + sb >= 2:
                    pe.wait_ge(s_o, 2 * h + sb - 1)
                w = V[:, j, h // 2, HD * (h % 2):HD * (h % 2) + P]
                pe.matmul(ps[:, 6 + sb, P * c:HALF], w, prob[:, k % 4, P * c:HALF], start=(j == 0),
                          stop=(j == 4 * sb + 3), skip_group_check=True).then_inc(s_pv, 1)

            def group_sums(t):
                pe.wait_ge(s_ysq, t + 1)
                for half in range(2):
                    bank = st_slot(ST_AT[(t, SUMS, half)])
                    pe.matmul(ps[:, bank, :], pairs[:], ysq[:, HALF * half:HALF * half + HALF], start=True,
                              stop=True).then_inc(s_yss, 1)

            pe.wait_ge(s_vones, 5)
            pe.wait_ge(s_mask, len(IDX_BLOCKS))
            logits(0)
            maxima(0)
            for h in range(NH):
                first = PV_AT[(h, 0, 0)]
                count = len(chunks(0)) + len(chunks(1))
                for x in range(count):
                    scores_t(ST_AT[PV[first + x][:3]])
                    if x >= 1:
                        values(first + x - 1)
                if h in SUMS_AFTER and h < NH - 1:
                    group_sums(SUMS_AFTER[h])
                if h + 1 < NH:
                    logits(h + 1)
                values(first + count - 1)
                if h + 1 < NH:
                    maxima(h + 1)
            pe.wait_ge(s_gacc, KT)
            pe.wait_ge(s_onesq, 1)
            pe.wait_ge(s_mx, NB * NH)
            for half in range(2):
                mm = pe.matmul(ps[:, 2 + half, :], onesq[:], gate[:, HALF * half:HALF * half + HALF], start=True, stop=True)
            mm.then_inc(s_gp, 1)
            group_sums(NT - 1)

            pe.wait_ge(s_woLp, KT // 2)
            pe.wait_ge(s_woLd, KT // 2)
            pe.wait_ge(s_woH, KT)
            for b in range(NB):
                if b == 1:
                    pe.wait_ge(s_gate, 1)
                if b >= 2:
                    pe.wait_ge(s_og, b - 1)
                for part in range(2):
                    pe.wait_ge(s_yH, 2 * b + part + 1)
                    pe.wait_ge(s_yL, 2 * b + part + 1)
                    for half in range(2):
                        out = ps[:, 2 * (b % 2) + half, :]
                        cols = slice(HALF * half, HALF * half + HALF)
                        for ct in range(NT * part, NT * part + NT):
                            pe.matmul(out, yH[b % 2][:, ct, :], hH[:, ct, cols], start=(ct == 0), stop=False)
                            pe.matmul(out, yH[b % 2][:, ct, :], hL[:, ct, cols], start=False, stop=False)
                            mm = pe.matmul(out, yL[b % 2][:, ct, :], hH[:, ct, cols], start=False, stop=(ct == KT - 1))
                mm.then_inc(s_op, 1)

        @block.scalar
        def _(act):
            A = nc.scalar.activation
            act.wait_ge(s_const, 16 * 4)
            A(csilu, vec[:, V_C:V_C + KT], ACT.Silu).then_inc(s_csilu, 1)
            for t in range(NB):
                act.wait_ge(s_x[t], 16)
                if t >= 4:
                    act.wait_ge(s_sumsq, t - 3)
                A(two(2 * (t % 4)), xin[:, t, :], ACT.Square, accum_out=sumsq[:, t:t + 1]).then_inc(s_sumsq, 1)
            act.wait_ge(s_var, 1)
            A(rstd, sumsq, ACT.Sqrt).then_inc(s_std, 1)
            for kt in range(KT):
                act.wait_ge(s_xtp, kt + 1)
                A(xT[:, kt, :], two(2 * (kt % 4)), ACT.Copy).then_inc(s_xt, 1)

            def split_high(n):
                act.wait_ge(s_raw[n % NRAW], 16 * (n // NRAW + 1))
                if n < NU:
                    if n >= 2:
                        act.wait_ge(s_unit, n - 1)
                    m = 72 if n == 0 else P
                    A(wH[:, n % 2, :, 0:m], raw[:, n % NRAW, :, 0:m], ACT.Copy).then_inc(s_wH, 1)
                else:
                    act.wait_ge(s_unit, NU)
                    A(hH[:, n - NU, :], raw[:, n % NRAW, :, :].rearrange("p k n -> p (k n)"), ACT.Copy).then_inc(s_woH, 1)

            split_high(0)
            split_high(1)
            for kt in range(KT):
                act.wait_ge(s_h, kt + 1)
                A(hH[:, kt, :], xT[:, kt, :], ACT.Copy).then_inc(s_hH, 1)
            act.wait_ge(s_red, 1)
            A(tabS[:], ang[:], ACT.Sin).then_inc(s_trig, 1)
            A(turns[:], ang[:], ACT.Abs).then_inc(own_act, 1)
            act.wait_ge(s_red, 2)
            A(tabC[:], turns[:], ACT.Sin).then_inc(s_trig, 1)

            def evacuate(n):
                sec, t = UNITS[n]
                act.wait_ge(s_unit, n + 1)
                src = two(2 * (n % 2))
                if sec == "ik":
                    A(Tik[0:72, :], src[0:72, :], ACT.Copy).then_inc(s_evac, 1)
                elif sec in SECT:
                    if sec == "aq" and t == 0:
                        act.wait_ge(s_splL, NT)
                    if sec == "ak" and t == 0:
                        act.wait_ge(s_splL, 2 * NT)
                    A(T[:, t, :], src, ACT.Copy).then_inc(s_evac, 1)
                elif sec == "av":
                    if t == 0:
                        act.wait_ge(s_idx, NIH * len(IDX_BLOCKS))
                    if t >= 2:
                        act.wait_ge(s_vt, t - 1)
                    A(vst[:, t % 2, :], src, ACT.Copy).then_inc(s_evac, 1)
                elif sec == "cc":
                    if t >= 1:
                        act.wait_ge(s_cvs, t)
                    A(convc[:], src, ACT.Copy).then_inc(s_evac, 1)
                elif sec == "cu":
                    A(convu[:], src, ACT.Copy).then_inc(s_evac, 1)
                elif sec == "cb":
                    if t == 0:
                        act.wait_ge(s_splL, 3 * NT)
                    else:
                        act.wait_ge(s_cvn, t)
                    A(convb[:], src, ACT.Copy).then_inc(s_evac, 1)
                elif sec == "cz":
                    if t == 0:
                        act.wait_ge(s_spill[0], 16 * 24)
                        act.wait_ge(s_spill[1], 16 * 24)
                    A(yconv[:, t, :], src, ACT.Silu).then_inc(s_evac, 1)
                elif sec == "az":
                    A(azs[:, t, :], src, ACT.Silu).then_inc(s_evac, 1)

            def taps(t):
                act.wait_ge(s_cvs, t + 1)
                A(conv0[:], convs[:, 2:2 + S], ACT.Identity, bias=vec[:, V_CB + t:V_CB + t + 1],
                  scale=vec[:, V_CW + 8 + t:V_CW + 9 + t]).then_inc(s_cvt, 1)
                A(conv1[:], convs[:, 1:1 + S], ACT.Copy, scale=vec[:, V_CW + 4 + t:V_CW + 5 + t]).then_inc(s_cvt, 1)
                act.wait_ge(s_cvy, 2 * t + 1)
                A(conv1[:], convs[:, 0:S], ACT.Copy, scale=vec[:, V_CW + t:V_CW + 1 + t]).then_inc(s_cvt, 1)

            for kind, n in SCHEDULE:
                if kind == "unit":
                    evacuate(n)
                    if n + 2 < NU:
                        split_high(n + 2)
                    sec, t = UNITS[n]
                    if sec == "cb":
                        taps(t)
                    if sec == "cz":
                        act.wait_ge(s_cvy, 2 * t + 2)
                        A(conv0[:], convb[:], ACT.Square).then_inc(s_cvq, 1)
                    if UNITS[n] == ("iq", 1):
                        act.wait_ge(s_back, 16)
                        A(iks1[0:HD, :], Tik[0:HD, :], ACT.Copy).then_inc(s_kiH, 1)
                elif kind == "idx":
                    for h in range(NIH):
                        u = NIH * (n - 2) + h
                        act.wait_ge(s_idx, u + 1)
                        if u >= 2:
                            act.wait_ge(s_score, u - 1)
                        w = (n + 1) * P
                        A(relu[:, u % 2, 0:w], two(4 + 2 * (u % 2))[:, 0:w], ACT.Relu, scale=wabs[:, n, h:h + 1]).then_inc(s_relu, 1)
                elif kind == "vt":
                    act.wait_ge(s_vt, n + 1)
                    src = two(4 + 2 * (n % 2)).rearrange("p (b g d) -> p b g d", b=NB, g=2)
                    for g in range(2):
                        mm = A(V[:, :, n, 2 * HD * g:2 * HD * g + HD], src[:, :, g, :], ACT.Copy)
                    mm.then_inc(s_v, 1)
                elif kind == "cn":
                    act.wait_ge(s_cvp, n + 1)
                    A(conv1[:], two(4), ACT.Ln, scale=1.0 / HD, bias=vec[:, V_EPS:V_EPS + 1]).then_inc(s_cvd, 1)
                    act.wait_ge(s_cvd, n + 1)
                    A(conv1[:], conv1[:], ACT.Exp, scale=-0.5).then_inc(s_cvr, 1)
                if (kind, n) in SPLITS:
                    sec = SPLITS[(kind, n)]
                    for t in range(NT):
                        m = NT * SECT[sec] + t
                        if t == 0:
                            act.wait_ge(s_back, 16 + 32 * (SECT[sec] + 1))
                            if sec == "aq":
                                act.wait_ge(s_score, NIH * len(IDX_BLOCKS))
                        if m >= 2:
                            act.wait_ge(s_spill[m % 2], 64 * (m // 2))
                        A(hl[m % 2][:, 0, :], T[:, t, :], ACT.Copy).then_inc(s_splH, 1)

            for n in range(NU, NU + KT):
                split_high(n)

            def exps(h):
                for sb in range(2):
                    for j, c in chunks(sb):
                        k = PV_AT[(h, sb, j)]
                        act.wait_ge(s_st, k + 1)
                        if k == 0:
                            act.wait_ge(s_vt, NT)
                        if k >= 4:
                            act.wait_ge(s_pv, k - 3)
                        A(prob[:, k % 4, P * c:HALF], ps[:, 4 + ST_AT[(h, sb, j)] % 2, P * c:HALF], ACT.Exp,
                          scale=ATT_SCALE).then_inc(s_exp, 1)

            def pair_rstd(t):
                for half in range(2):
                    act.wait_ge(s_yss, 2 * t + half + 1)
                    z = ysq[:, HALF * half:HALF * half + HALF]
                    A(z, ps[:, 4 + ST_AT[(t, SUMS, half)] % 2, :], ACT.Ln, scale=1.0 / HD,
                      bias=vec[:, V_EPS:V_EPS + 1]).then_inc(s_yln, 1)
                    act.wait_ge(s_yln, 2 * t + half + 1)
                    A(z, z, ACT.Exp, scale=-0.5).then_inc(s_yrs, 1)

            def high(b, part):
                if b >= 2:
                    act.wait_ge(s_op, b - 1)
                if part:
                    act.wait_ge(s_ya, NT)
                A(yH[b % 2][:, NT * part:NT * part + NT, :], (yconv, ya)[part][:, :, P * b:P * b + P], ACT.Copy).then_inc(s_yH, 1)

            for h in range(NH):
                exps(h)
                if h == NH - 1:
                    act.wait_ge(s_pv, len(PV))
                    high(0, 0)
                if h in SUMS_AFTER:
                    pair_rstd(SUMS_AFTER[h])
            high(0, 1)
            high(1, 0)
            high(1, 1)
            for b in range(NB):
                if b + 2 < NB:
                    high(b + 2, 0)
                    high(b + 2, 1)
                act.wait_ge(s_res, b + 1)
                if b >= 2:
                    act.wait_ge(s_out[b % 2], 16 * (b // 2))
                A(oe[:, b % 2, :], te[:, b % 2, :], ACT.Square, accum_out=fin[:, b:b + 1]).then_inc(s_fsq, 1)
                act.wait_ge(s_fv, b + 1)
                A(finr[:, b:b + 1], fin[:, b:b + 1], ACT.Sqrt).then_inc(s_fs, 1)

        @block.vector
        def _(dve):
            v = nc.vector
            chain = [0]

            def link(ins):
                chain[0] += 1
                ins.then_inc(own_dve, 1)
                dve.wait_ge(own_dve, chain[0])

            v.memset(onesF[:], 1.0).then_inc(s_ones, 1)
            dve.wait_ge(s_sumsq, NB)
            v.tensor_scalar(sumsq, sumsq, 1.0 / D, EPS, ALU.mult, ALU.add).then_inc(s_var, 1)
            dve.wait_ge(s_std, 1)
            link(v.reciprocal(rstd, rstd))
            for t in range(NB):
                v.tensor_scalar(xin[:, t, :], xin[:, t, :], rstd[:, t:t + 1], None, ALU.mult).then_inc(s_xn, 1)
            dve.wait_ge(s_csilu, 1)
            for kt in range(KT):
                dve.wait_ge(s_wa[kt % 4], 16 * (kt // 4 + 1))
                if kt == 0:
                    v.tensor_scalar(acc[:], wa[0][:], csilu[:, 0:1], None, ALU.mult).then_inc(s_acc, 1)
                else:
                    dve.wait_ge(s_acc, kt)
                    v.scalar_tensor_tensor(acc[:], wa[kt % 4][:], csilu[:, kt:kt + 1], acc[:], ALU.mult, ALU.add).then_inc(s_acc, 1)
            dve.wait_ge(s_modp, 1)
            v.tensor_tensor(shift, ps[:, 0, 0:KT], vec[:, V_BSH:V_BSH + KT], ALU.add)
            link(v.tensor_tensor(amp, ps[:, 0, KT:2 * KT], vec[:, V_BSC:V_BSC + KT], ALU.add))
            link(v.scalar_tensor_tensor(amp, amp, 1.0, vec[:, V_NORM:V_NORM + KT], ALU.add, ALU.mult))
            for kt in range(KT):
                dve.wait_ge(s_xt, kt + 1)
                v.tensor_scalar(xT[:, kt, :], xT[:, kt, :], amp[:, kt:kt + 1], shift[:, kt:kt + 1], ALU.mult, ALU.add).then_inc(s_h, 1)
                dve.wait_ge(s_h, kt + 1)
                dve.wait_ge(s_hH, kt + 1)
                v.tensor_tensor(hL[:, kt, :], xT[:, kt, :], hH[:, kt, :].bitcast(F32), ALU.subtract).then_inc(s_hL, 1)

            dve.wait_ge(s_pos, 16)
            link(v.tensor_copy(ang[:], posi[:]))
            link(v.tensor_scalar(ang[:], ang[:], vec[:, V_FREQ:V_FREQ + 1], None, ALU.mult))
            link(v.tensor_scalar(turns[:], ang[:], 1.0 / (2 * np.pi), MAGIC, ALU.mult, ALU.add))
            link(v.tensor_scalar(turns[:], turns[:], MAGIC, None, ALU.subtract))
            for part in two_pi_parts():
                link(v.scalar_tensor_tensor(ang[:], turns[:], -part, ang[:], ALU.mult, ALU.add))
            v.tensor_scalar(ang[:], ang[:], PI, -PI, ALU.min, ALU.max).then_inc(s_red, 1)
            dve.wait_ge(own_act, 1)
            v.tensor_scalar(turns[:], turns[:], -1.0, float(np.pi / 2), ALU.mult, ALU.add).then_inc(s_red, 1)
            dve.wait_ge(s_trig, 2)
            v.tensor_scalar(tabS[:], tabS[:], vec[:, V_SIGN:V_SIGN + 1], None, ALU.mult).then_inc(s_tab, 1)
            dve.wait_ge(s_tab, 1)

            def rotate(k, n, count):
                dve.wait_ge(s_cx, count)
                v.tensor_tensor(cx[0:n, :], cx[0:n, :], tabC[0:n, :], ALU.mult)
                link(v.tensor_tensor(cs[0:n, :], cs[0:n, :], tabS[0:n, :], ALU.mult))
                v.tensor_tensor(cx[0:n, :], cx[0:n, :], cs[0:n, :], ALU.add).then_inc(s_rot, 1)

            rotate(0, ROPE, 48)
            dve.wait_ge(s_iwt, 1)
            iwp = ps[:, 4, 0:NB * NIH]
            wf = wabs[:].rearrange("p b h -> p (b h)")
            wg = wsgn[:].rearrange("p b h -> p (b h)")
            link(v.tensor_scalar(wg, iwp, 0.0, 2.0, ALU.is_ge, ALU.mult))
            link(v.tensor_scalar(wg, wg, 1.0, None, ALU.subtract))
            v.scalar_tensor_tensor(wf, iwp, IDX_SCALE, wg, ALU.mult, ALU.mult).then_inc(s_iw, 1)
            dve.wait_ge(s_kiH, 1)
            v.tensor_tensor(iks2[0:HD, :], Tik[0:HD, :], iks1[0:HD, :].bitcast(F32), ALU.subtract).then_inc(s_kiL, 1)
            rotate(1, P, 48 + 32)
            for t in range(NT):
                section_low(v, dve, "iq", t)
            dve.wait_ge(s_iw, 1)
            for i in IDX_BLOCKS:
                n = (i + 1) * P
                for h in range(NIH):
                    u = NIH * (i - 2) + h
                    dve.wait_ge(s_relu, u + 1)
                    if h == 0:
                        v.tensor_scalar(score_of(i), relu[:, u % 2, 0:n], wsgn[:, i, 0:1], None, ALU.mult).then_inc(s_score, 1)
                    else:
                        dve.wait_ge(s_score, u)
                        v.scalar_tensor_tensor(score_of(i), relu[:, u % 2, 0:n], wsgn[:, i, h:h + 1], score_of(i),
                                               ALU.mult, ALU.add).then_inc(s_score, 1)

            def top_keys(i):
                dve.wait_ge(s_caus, i - 1)
                sc = score_of(i)
                with dve.Fori(0, TOPK // ROUND // 8):
                    for r in range(8):
                        if r:
                            dve.wait_ge(s_round, 2 * r)
                        v.max(m8[:], sc).then_inc(s_round, 1)
                        dve.wait_ge(s_round, 2 * r + 1)
                        v.match_replace(sc, m8[:], sc, TAKEN).then_inc(s_round, 1)
                    dve.wait_ge(s_round, 16)
                    dve.sem_clear(s_round)
                v.tensor_scalar(bias_of(i), sc, TAKEN, -BIG, ALU.not_equal, ALU.mult).then_inc(s_mask, 1)

            rotate(2, P, 48 + 64)
            top_keys(2)
            top_keys(3)
            rotate(3, P, 48 + 96)
            for i in range(4, NB):
                top_keys(i)
            for c in range(1, KT, 2):
                out_low(v, dve, c, s_woLd)
            dve.wait_ge(s_mask, len(IDX_BLOCKS))
            dve.wait_ge(s_vones, 5)

            def row_max(h):
                for i in range(NB):
                    u = NB * h + i
                    dve.wait_ge(s_lg, u + 1)
                    src = two(2 * (u % 2))[:, 0:(i + 1) * P]
                    v.tensor_tensor_reduce(src, src, bias_of(i), 1.0, -3.0e38, ALU.add, ALU.max, mx[:, i:i + 1]).then_inc(s_mx, 1)
                dve.wait_ge(s_mx, NB * (h + 1))
                if h >= 1:
                    dve.wait_ge(s_mt, h)
                link(v.tensor_scalar(mparts[:, 0:NB], mx[:], -1.0, None, ALU.mult))
                v.scalar_tensor_tensor(mparts[:, NB:2 * NB], mx[:], -1.0, mparts[:, 0:NB], ALU.mult, ALU.subtract).then_inc(s_mp, 1)

            def max_rows(h):
                dve.wait_ge(s_mt, h + 1)
                if h == 0:
                    dve.wait_ge(s_delta, 16)
                else:
                    dve.wait_ge(s_st, PV_AT[(h - 1, 1, NB - 1)] + 1)
                src = ps[0:16, 4 + ST_AT[(h, -1, 0)] % 2, :].bitcast(BF16)[:, 0:P]
                v.tensor_tensor(mrow[:], src.rearrange("p (o n) -> p o n", o=1).broadcast_to([16, NB, P]), delta[:],
                                ALU.mult).then_inc(s_mrow, 1)

            def head_out(h, sb):
                dve.wait_ge(s_pv, PV_AT[(h, sb, 4 * sb + 3)] + 1)
                r, d = rows(h), rows(h + 1)
                if 2 * h + sb:
                    dve.wait_ge(s_o, 2 * h + sb)
                link(v.reciprocal(rden[r, :], ps[d, 6 + sb, :]))
                v.tensor_tensor(ya[r, h // 2, HALF * sb:HALF * sb + HALF], ps[r, 6 + sb, :], rden[r, :], ALU.mult).then_inc(s_o, 1)

            def gate_sum(kt):
                dve.wait_ge(s_gw[kt % 2], 16 * (kt // 2 + 1))
                if kt == 0:
                    v.tensor_scalar(gate[:], gw[:, 0, :], csilu[:, 0:1], None, ALU.mult).then_inc(s_gacc, 1)
                else:
                    dve.wait_ge(s_gacc, kt)
                    v.scalar_tensor_tensor(gate[:], gw[:, kt % 2, :], csilu[:, kt:kt + 1], gate[:], ALU.mult, ALU.add).then_inc(s_gacc, 1)

            def pair_gate(t):
                dve.wait_ge(s_yn, t + 1)
                v.scalar_tensor_tensor(ya[:, t, :], ya[:, t, :], vec[:, V_GA + t:V_GA + t + 1], azs[:, t, :],
                                       ALU.mult, ALU.mult).then_inc(s_ya, 1)

            def low_y(b, part):
                dve.wait_ge(s_yH, 2 * b + part + 1)
                k = slice(NT * part, NT * part + NT)
                v.tensor_tensor(yL[b % 2][:, k, :], (yconv, ya)[part][:, :, P * b:P * b + P],
                                yH[b % 2][:, k, :].bitcast(F32), ALU.subtract).then_inc(s_yL, 1)

            row_max(0)
            max_rows(0)
            dve.wait_ge(s_woLp, KT // 2)
            dve.wait_ge(s_woH, KT)
            for h in range(NH):
                head_out(h, 0)
                if h + 1 < NH:
                    row_max(h + 1)
                head_out(h, 1)
                if 1 <= h <= 4:
                    gate_sum(2 * h - 2)
                    gate_sum(2 * h - 1)
                if h + 1 < NH:
                    max_rows(h + 1)
                if h in (3, 5, 7):
                    pair_gate(h // 2 - 1)
            low_y(0, 0)
            dve.wait_ge(s_gp, 1)
            dve.wait_ge(s_nf, 32)
            v.tensor_tensor(gate[:], two(2), bgate[:], ALU.add).then_inc(s_gate, 1)
            pair_gate(NT - 1)
            low_y(0, 1)
            low_y(1, 0)
            low_y(1, 1)
            dve.wait_ge(s_gate, 1)
            for b in range(NB):
                dve.wait_ge(s_op, b + 1)
                if b >= 2:
                    dve.wait_ge(s_fin, b - 1)
                v.tensor_tensor(te[:, b % 2, :], two(2 * (b % 2)), gate[:], ALU.mult).then_inc(s_og, 1)
                if b + 2 < NB:
                    low_y(b + 2, 0)
                    low_y(b + 2, 1)
                dve.wait_ge(s_fsq, b + 1)
                v.tensor_scalar(fin[:, b:b + 1], fin[:, b:b + 1], 1.0 / D, EPS, ALU.mult, ALU.add).then_inc(s_fv, 1)
                dve.wait_ge(s_fs, b + 1)
                link(v.reciprocal(finr[:, b:b + 1], finr[:, b:b + 1]))
                if b >= 2:
                    dve.wait_ge(s_out[b % 2], 16 * (b // 2))
                v.scalar_tensor_tensor(oe[:, b % 2, :], te[:, b % 2, :], finr[:, b:b + 1], normf[:], ALU.mult, ALU.mult).then_inc(s_fin, 1)

        @block.gpsimd
        def _(pool):
            g = nc.gpsimd
            g.memset(onesB[:], 1.0).then_inc(s_vones, 1)

            def split_low(n):
                m = 72 if n == 0 else P
                pool.wait_ge(s_wH, n + 1)
                g.tensor_tensor(wL[:, n % 2, :, 0:m], raw[:, n % NRAW, :, 0:m], wH[:, n % 2, :, 0:m].bitcast(F32),
                                ALU.subtract).then_inc(s_wL, 1)

            split_low(0)
            split_low(1)
            for kind, n in SCHEDULE:
                if kind == "unit":
                    sec, t = UNITS[n]
                    if sec != "cb" and n + 2 < NU:
                        split_low(n + 2)
                    if sec == "cb":
                        pool.wait_ge(s_evac, UNIT[("cu", t)] + 1)
                        if t == 0:
                            pool.wait_ge(s_splL, 3 * NT)
                            g.memset(convs[:, 0:2], 0.0).then_inc(s_pad, 1)
                        g.tensor_tensor(convs[:, 2:2 + S], convc[:], convu[:], ALU.mult).then_inc(s_cvs, 1)
                        split_low(n + 2)
                        pool.wait_ge(s_cvt, 3 * t + 2)
                        g.tensor_tensor(conv0[:], conv0[:], conv1[:], ALU.add).then_inc(s_cvy, 1)
                        pool.wait_ge(s_cvt, 3 * t + 3)
                        pool.wait_ge(s_cvy, 2 * t + 1)
                        g.tensor_tensor(conv0[:], conv0[:], conv1[:], ALU.add).then_inc(own_pool, 1)
                        pool.wait_ge(own_pool, 3 * t + 1)
                        pool.wait_ge(s_evac, n + 1)
                        g.tensor_tensor(convb[:], convb[:], conv0[:], ALU.mult).then_inc(s_cvy, 1)
                elif kind == "idx":
                    pool.wait_ge(s_score, NIH * (n - 1))
                    d = score_of(n)[:, P * n:P * n + P]
                    g.affine_select(out=d, in_=d, compare_op=ALU.is_ge, fill=FUTURE, base=0, pattern=[[-1, P]],
                                    channel_multiplier=1).then_inc(s_caus, 1)
                elif kind == "cn":
                    pool.wait_ge(s_cvr, n + 1)
                    pool.wait_ge(s_cvy, 2 * n + 2)
                    g.tensor_tensor(convb[:], convb[:], conv1[:], ALU.mult).then_inc(own_pool, 1)
                    pool.wait_ge(own_pool, 3 * n + 2)
                    g.tensor_scalar(convb[:], convb[:], vec[:, V_GC + n:V_GC + n + 1], None, ALU.mult).then_inc(own_pool, 1)
                    pool.wait_ge(own_pool, 3 * n + 3)
                    pool.wait_ge(s_evac, UNIT[("cz", n)] + 1)
                    g.tensor_tensor(yconv[:, n, :], yconv[:, n, :], convb[:], ALU.mult).then_inc(s_cvn, 1)
                if (kind, n) == ("unit", 5):
                    g.memset(bias[:, 0:3 * P], 0.0).then_inc(s_vones, 1)
                    pool.wait_ge(s_vones, 2)
                    for i in range(2):
                        d = bias_of(i)[:, P * i:P * i + P]
                        g.affine_select(out=d, in_=d, compare_op=ALU.is_ge, fill=-BIG, base=0, pattern=[[-1, P]],
                                        channel_multiplier=1).then_inc(s_vones, 1)
                if (kind, n) == ("unit", UNIT[("av", 0)]):
                    pool.wait_ge(s_idx, NIH * len(IDX_BLOCKS))
                    g.memset(V[:, :, :, HD:2 * HD], 1.0).then_inc(s_vones, 1)
                if SPLITS.get((kind, n), "iq") != "iq":
                    for t in range(NT):
                        section_low(g, pool, SPLITS[(kind, n)], t)
            for c in range(0, KT, 2):
                out_low(g, pool, c, s_woLp)

            def pair_square(t):
                pool.wait_ge(s_o, 4 * (t + 1))
                if t == 0:
                    g.memset(onesq[:], 1.0).then_inc(s_onesq, 1)
                else:
                    pool.wait_ge(s_yn, t)
                g.tensor_tensor(ysq[:], ya[:, t, :], ya[:, t, :], ALU.mult).then_inc(s_ysq, 1)

            def pair_scale(t):
                pool.wait_ge(s_yrs, 2 * t + 2)
                g.tensor_tensor(ya[:, t, :], ya[:, t, :], ysq[:], ALU.mult).then_inc(s_yn, 1)

            for t in range(NT):
                pair_square(t)
                pair_scale(t)
            for b in range(NB):
                pool.wait_ge(s_og, b + 1)
                pool.wait_ge(s_xe[b % 2], 16 * (b // 2 + 1))
                g.tensor_tensor(te[:, b % 2, :], te[:, b % 2, :], xe[:, b % 2, :], ALU.add).then_inc(s_res, 1)


INPUTS = ("x", "positions", "w_ada", "w_out", "norm_f", "b_gate", "w_ik", "w_units", "vecs", "ident_f", "ident_b",
          "pairs", "delta")


def kernel(x, c, positions, w_ada, b_ada, norm_in, w_in, conv_w, conv_b, gn_conv, gn_attn, w_out, norm_f):
    import ml_dtypes
    import concourse.bacc as bacc
    from concourse.bass_utils import run_bass_kernel_spmd

    def columns(v):
        return np.asarray(v).reshape(-1, P).T

    w_in = np.asarray(w_in)
    tiles = np.stack([w_in[:, STARTS[s] + P * t:STARTS[s] + P * t + P] for s, t in UNITS[1:]])
    freq = np.float32(500000.0) ** (-np.arange(ROPE // 2, dtype=np.float32) / np.float32(ROPE // 2))
    row = np.arange(P) % ROPE
    vecs = np.zeros((P, V_COLS), np.float32)
    for at, v in ((V_C, c), (V_NORM, norm_in), (V_BSH, b_ada[:D]), (V_BSC, b_ada[D:2 * D]), (V_CW, conv_w),
                  (V_CB, conv_b), (V_GC, gn_conv), (V_GA, gn_attn)):
        v = columns(v)
        vecs[:, at:at + v.shape[1]] = v
    vecs[:, V_FREQ] = freq[row % (ROPE // 2)]
    vecs[:, V_SIGN] = np.where(row < ROPE // 2, -1.0, 1.0)
    vecs[:, V_EPS] = EPS
    group = np.arange(P) // HD
    arrays = {
        "x": x, "positions": positions, "w_ada": w_ada, "w_out": w_out, "norm_f": norm_f, "b_gate": b_ada[2 * D:],
        "w_ik": w_in[:, 4608:4680].reshape(KT, P, 72).transpose(1, 0, 2),
        "w_units": tiles.reshape(NU - 1, KT, P, P).transpose(0, 2, 1, 3),
        "vecs": vecs, "ident_f": np.eye(P, dtype=np.float32), "ident_b": np.eye(P).astype(ml_dtypes.bfloat16),
        "pairs": (group[:, None] == group[None, :]).astype(np.float32),
        "delta": (np.arange(16)[:, None, None] % NB == np.arange(NB)[None, :, None]).repeat(P, 2).astype(ml_dtypes.bfloat16),
    }
    arrays = {"in_" + k: np.ascontiguousarray(arrays[k]) for k in INPUTS}
    nc = bacc.Bacc("TRN2", target_bir_lowering=False, num_devices=1)
    aps = {k: nc.dram_tensor("in_" + k, arrays["in_" + k].shape, mybir.dt.from_np(arrays["in_" + k].dtype),
                             kind="ExternalInput").ap() for k in INPUTS}
    aps["out"] = nc.dram_tensor("out", (1, S, D), F32, kind="ExternalOutput").ap()
    build(nc, aps)
    return run_bass_kernel_spmd(nc, [arrays], core_ids=[0]).results[0]["out"]
```

```python
from contextlib import ExitStack

import numpy as np

import concourse.bass as bass
from concourse import mybir

P = 128
D = 1024
S = 1024
KT = D // P
NB = S // P
HD = 64
NH = 8
NIH = 8
NT = 4
ROPE = 16
TOPK = 256
ROUND = 8
HALF = 512
EPS = 1e-6
IDX_SCALE = float(HD) ** -0.5 * float(NIH) ** -0.5
ATT_SCALE = float(HD) ** -0.5
TAKEN = -3.0e38
FUTURE = -3.3e38
BIG = 1.0e30
MAGIC = 1.5 * 2.0 ** 23
PI = 3.1415925

F32 = mybir.dt.float32
F32R = mybir.dt.float32r
BF16 = mybir.dt.bfloat16
I32 = mybir.dt.int32
ALU = mybir.AluOpType
ACT = mybir.ActivationFunctionType

V_C, V_NORM, V_BSH, V_BSC = 0, 8, 16, 24
V_CW, V_CB, V_GC, V_GA = 32, 44, 48, 52
V_FREQ, V_SIGN, V_EPS, V_COLS = 56, 57, 58, 64


def two_pi_parts():
    left, parts = 2 * np.pi, []
    for _ in range(3):
        m, e = np.frexp(left)
        parts.append(float(np.round(m * 256) / 256 * 2.0 ** e))
        left -= parts[-1]
    return parts + [float(left)]


UNITS = ([("ik", 0)] + [("aq", t) for t in range(NT)] + [("iq", t) for t in range(NT)]
         + [("ak", t) for t in range(NT)] + [("av", t) for t in range(NT)]
         + [(s, t) for t in range(NT) for s in ("cc", "cu", "cb", "cz")] + [("az", t) for t in range(NT)])
NU = len(UNITS)
UNIT = {u: n for n, u in enumerate(UNITS)}
STARTS = {s: 512 * i for i, s in enumerate(("cb", "cc", "cu", "cz", "aq", "ak", "av", "az", "iq"))}
NRAW = 2


def schedule():
    after = {
        ("aq", 0): [("iwt", 0)],
        ("ak", 2): [("idx", 2), ("idx", 3)],
        ("ak", 3): [("idx", 4), ("idx", 5), ("idx", 6), ("idx", 7)],
        ("av", 2): [("vt", 0)],
        ("av", 3): [("vt", 1)],
        ("cc", 0): [("vt", 2)],
        ("cu", 0): [("vt", 3)],
    }
    for t in range(NT):
        n = UNIT[("cz", t)] + 1
        after.setdefault(UNITS[n], []).append(("cn", t))
    out = []
    for n, u in enumerate(UNITS):
        out.append(("unit", n))
        out += after.get(u, [])
    return out


SCHEDULE = schedule()
SPLITS = {("unit", UNIT[("iq", 1)]): "aq", ("unit", UNIT[("ak", 1)]): "iq", ("unit", UNIT[("cc", 0)]): "ak"}
SCORES_IN = {UNIT[("ak", 3)]: (2, 8), UNIT[("av", 0)]: (4, 0), UNIT[("av", 1)]: (6, 0)}
HL_POOL = (2, 5)
IDX_BLOCKS = range(TOPK // P, NB)
NI = len(IDX_BLOCKS)
HALVINGS = 10
SUMS_AFTER = {2: 0, 4: 1, 6: 2, 7: 3}


def build(nc, a):
    with ExitStack() as ctx:
        base = 16512
        used = [0]

        def at(name, shape, dt, kb):
            off = base + int(kb * 1024)
            assert off % 32 == 0
            return nc.alloc_sbuf_tensor_at(name, shape, dt, offset=off)

        def sem(name):
            return ctx.enter_context(nc.semaphore(name))

        arena = ctx.enter_context(nc.sbuf_tensor("arena", [P, 207 * 256], F32))

        hH = at("hH", [P, KT, S], F32R, 0)
        hL = at("hL", [P, KT, S], F32R, 32)
        raw = at("raw", [P, NRAW, KT, P], F32, 64)
        wH = at("wH", [P, 2, KT, P], F32R, 76)
        wL = at("wL", [P, 2, KT, P], F32R, 84)
        bias = at("bias", [P, 36 * P], BF16, 92)
        score = at("score", [P, 33 * P], F32, 93.5)
        identF = at("identF", [P, P], F32, 110)
        pairs = at("pairs", [P, P], F32, 110.5)
        identB = at("identB", [P, P], BF16, 111)
        onesB = at("onesB", [16, P], BF16, 111.25)
        vec = at("vec", [P, V_COLS], F32, 111.5)
        wabs = at("wabs", [P, NB, NIH], F32, 111.75)
        wsgn = at("wsgn", [P, NB, NIH], F32, 112)
        small = at("small", [P, 64], F32, 112.25)
        onesF = at("onesF", [P, 1], F32, 112.5)
        m8 = at("m8", [P, ROUND], F32, 112.5625)
        mx = at("mx", [P, NB], F32, 112.625)
        mparts = at("mparts", [P, 2 * NB], BF16, 112.6875)
        srch = at("srch", [P, 64], F32, 112.75)
        lo, step, hi, cand, count, good, need, most = (srch[:, NI * k:NI * k + NI] for k in range(8))
        ramp = srch[:, 48:48 + ROUND]
        limit = srch[:, 56:56 + ROUND]
        rounds = at("rounds", [P, NI], I32, 112.75)
        above = at("above", [P, S], BF16, 205)
        csilu = small[:, 0:8]
        sumsq = small[:, 8:16]
        rstd = small[:, 16:24]
        shift = small[:, 24:32]
        amp = small[:, 32:40]
        fin = small[:, 40:48]
        finr = small[:, 48:56]
        xin = at("xin", [P, NB, D], F32, 113)
        xT = at("xT", [P, KT, S], F32, 145)
        wa = [at(f"wa{i}", [P, 2 * D], F32, kb) for i, kb in enumerate((177, 185, 93, 101))]
        acc = at("acc", [P, 2 * D], F32, 193)
        iqs = at("iqs", [P, NIH, S], F32R, 113)
        iks1 = at("iks1", [P, S], F32R, 145)
        iks2 = at("iks2", [P, S], F32R, 149)
        Taqk = at("Taqk", [P, NT, S], F32, 153)
        Tiq = at("Tiq", [P, NT, S], F32, 93.5)
        T = {"iq": Tiq, "aq": Taqk, "ak": Taqk}
        cx = at("cx", [P, S], F32, 169)
        cs = at("cs", [P, S], F32, 173)
        tabC = at("tabC", [P, S], F32, 177)
        tabS = at("tabS", [P, S], F32, 181)
        Tik = at("Tik", [P, S], F32, 185)
        hlH = [at(f"hlH{i}", [P, S], F32R, kb) for i, kb in enumerate((189, 72))]
        hlL = [at(f"hlL{i}", [P, S], F32R, kb) for i, kb in enumerate((193, 185))]
        relu = at("relu", [P, 2, S], F32, 197)
        posi = at("posi", [P, S], I32, 169)
        ang = at("ang", [P, S], F32, 173)
        turns = at("turns", [P, S], F32, 189)
        V = at("V", [P, NB, NT, 3 * HD], F32, 113)
        vst = at("vst", [P, 2, S], F32, 137)
        convc = at("convc", [P, S], F32, 145)
        convu = at("convu", [P, S], F32, 149)
        convs = at("convs", [P, 2 + S], F32, 153)
        conv0 = at("conv0", [P, S], F32, 157.25)
        conv1 = at("conv1", [P, S], F32, 161.5)
        convb = at("convb", [P, S], F32, 165.5)
        azs = at("azs", [P, NT, S], F32, 170)
        yconv = at("yconv", [P, NT, S], F32, 189)
        qs = [at(f"qs{i}", [P, S], F32R, 145 + 12 * i) for i in range(2)]
        ks1 = [at(f"ks1_{i}", [P, S], F32R, 149 + 12 * i) for i in range(2)]
        ks2 = [at(f"ks2_{i}", [P, S], F32R, 153 + 12 * i) for i in range(2)]
        prob = at("prob", [P, 4, HALF], F32, 137)
        mrow = at("mrow", [16, NB, P], BF16, 186)
        delta = at("delta", [16, NB, P], BF16, 205)
        ya = at("ya", [P, NT, S], F32, 64)
        rden = at("rden", [P, HALF], F32, 102)
        ysq = at("ysq", [P, S], F32, 104)
        onesq = at("onesq", [P, P], F32, 108)
        gw = at("gw", [P, 2, D], F32, 80)
        gate = at("gate", [P, D], F32, 88)
        yH = [at(f"yH{i}", [P, KT, P], F32R, 145 + 8 * i) for i in range(2)]
        yL = [at(f"yL{i}", [P, KT, P], F32R, 149 + 8 * i) for i in range(2)]
        normf = at("normf", [P, D], F32, 161)
        bgate = at("bgate", [P, D], F32, 165)
        xe = at("xe", [P, 2, D], F32, 113)
        oe = at("oe", [P, 2, D], F32, 121)
        te = at("te", [P, 2, D], F32, 129)

        ps = ctx.enter_context(nc.psum_tensor("ps", [P, 8, HALF], F32))

        def two(b):
            return ps[:, b:b + 2, :].rearrange("p b n -> p (b n)")

        dx = nc.dram_tensor("rope_x", [3, NH, ROPE, S], F32).ap()
        dp = nc.dram_tensor("rope_partner", [3, NH, ROPE, S], F32).ap()
        dr = nc.dram_tensor("rope_rotated", [3, NH, ROPE, S], F32).ap()
        dqk = nc.dram_tensor("qk_halves", [2, 2, NT, P, S], F32).ap()

        s_const = sem("s_const"); s_pos = sem("s_pos")
        s_x = [sem(f"s_x{t}") for t in range(NB)]
        s_wa = [sem(f"s_wa{i}") for i in range(4)]
        s_ones = sem("s_ones"); s_csilu = sem("s_csilu"); s_sumsq = sem("s_sumsq")
        s_var = sem("s_var"); s_std = sem("s_std"); s_xn = sem("s_xn")
        s_xtp = sem("s_xtp"); s_xt = sem("s_xt")
        s_acc = sem("s_acc"); s_modp = sem("s_modp")
        s_h = sem("s_h"); s_hH = sem("s_hH"); s_hL = sem("s_hL"); s_hLp = sem("s_hLp")
        s_red = sem("s_red"); s_trig = sem("s_trig"); s_tab = sem("s_tab")
        s_raw = [sem(f"s_raw{i}") for i in range(NRAW)]
        s_wH = sem("s_wH"); s_wL = sem("s_wL")
        s_unit = sem("s_unit"); s_evac = sem("s_evac")
        s_iwt = sem("s_iwt"); s_iw = sem("s_iw")
        s_cx = sem("s_cx"); s_rot = sem("s_rot"); s_back = sem("s_back"); s_bounce = sem("s_bounce")
        s_kiH = sem("s_kiH"); s_kiL = sem("s_kiL"); s_kidup = sem("s_kidup")
        s_splH = sem("s_splH"); s_splL = sem("s_splL")
        s_spill = [sem("s_spill0"), sem("s_spill1")]
        s_idx = sem("s_idx"); s_relu = sem("s_relu"); s_score = sem("s_score")
        s_caus = sem("s_caus"); s_round = sem("s_round"); s_mask = sem("s_mask")
        s_range = sem("s_range"); s_halve = sem("s_halve"); s_count = sem("s_count"); s_need = sem("s_need")
        s_most = sem("s_most")
        s_vt = sem("s_vt"); s_v = sem("s_v"); s_vones = sem("s_vones")
        s_cvs = sem("s_cvs"); s_cvt = sem("s_cvt"); s_cvy = sem("s_cvy"); s_cvq = sem("s_cvq")
        s_cvp = sem("s_cvp"); s_cvd = sem("s_cvd"); s_cvr = sem("s_cvr"); s_cvn = sem("s_cvn")
        s_pad = sem("s_pad"); s_onesq = sem("s_onesq")
        s_woH = sem("s_woH"); s_woLp = sem("s_woLp"); s_woLd = sem("s_woLd")
        s_stack = [sem("s_stack0"), sem("s_stack1")]
        s_delta = sem("s_delta")
        s_lg = sem("s_lg"); s_mx = sem("s_mx"); s_mp = sem("s_mp"); s_mt = sem("s_mt"); s_mrow = sem("s_mrow")
        s_st = sem("s_st"); s_exp = sem("s_exp"); s_pv = sem("s_pv"); s_o = sem("s_o")
        s_ysq = sem("s_ysq"); s_yss = sem("s_yss"); s_yln = sem("s_yln"); s_yrs = sem("s_yrs")
        s_yn = sem("s_yn"); s_ya = sem("s_ya")
        s_gw = [sem("s_gw0"), sem("s_gw1")]
        s_gacc = sem("s_gacc"); s_gp = sem("s_gp"); s_gate = sem("s_gate"); s_nf = sem("s_nf")
        s_yH = sem("s_yH"); s_yL = sem("s_yL"); s_op = sem("s_op"); s_og = sem("s_og")
        s_xe = [sem("s_xe0"), sem("s_xe1")]
        s_res = sem("s_res"); s_fsq = sem("s_fsq"); s_fv = sem("s_fv"); s_fs = sem("s_fs")
        s_fin = sem("s_fin")
        s_out = [sem("s_out0"), sem("s_out1")]
        own_act = sem("own_act"); own_dve = sem("own_dve"); own_pool = sem("own_pool")

        SECT = {"aq": 0, "iq": 1, "ak": 2}
        NBOUNCE = 6

        def score_of(i):
            o = (i * (i + 1) // 2 - 3) * P
            return score[:, o:o + (i + 1) * P]

        def bias_of(i):
            o = (i * (i + 1) // 2) * P
            return bias[:, o:o + (i + 1) * P]

        def rows(h):
            return slice(HD * (h % 2), HD * (h % 2) + HD)

        def chunks(sb):
            return [(j, max(0, j - 4 * sb)) for j in range(4 * sb + 4)]

        MAXIMA, SUMS = -1, -2
        ST = []
        for h in range(NH):
            ST.append((h, MAXIMA, 0, 0))
            for sb in range(2):
                ST += [(h, sb, j, c) for j, c in chunks(sb)]
            if h in SUMS_AFTER:
                ST += [(SUMS_AFTER[h], SUMS, half, 0) for half in range(2)]
        ST_AT = {u[:3]: n for n, u in enumerate(ST)}
        PV = [u for u in ST if u[1] >= 0]
        PV_AT = {u[:3]: n for n, u in enumerate(PV)}

        def section_low(engine, waits, sec, t):
            m = NT * SECT[sec] + t
            waits.wait_ge(s_splH, m + 1)
            engine.tensor_tensor(hlL[m % 2][:], T[sec][:, t, :], hlH[m % 2][:].bitcast(F32),
                                 ALU.subtract).then_inc(s_splL, 1)

        def low_h(engine, waits, kt, done):
            waits.wait_ge(s_h, kt + 1)
            waits.wait_ge(s_hH, kt + 1)
            engine.tensor_tensor(hL[:, kt, :], xT[:, kt, :], hH[:, kt, :].bitcast(F32), ALU.subtract).then_inc(done, 1)

        def out_low(engine, waits, c, done):
            waits.wait_ge(s_woH, c + 1)
            engine.tensor_tensor(hL[:, c, :], raw[:, (NU + c) % NRAW, :, :].rearrange("p k n -> p (k n)"),
                                 hH[:, c, :].bitcast(F32), ALU.subtract).then_inc(done, 1)

        block = ctx.enter_context(nc.Block())

        @block.sync
        def _(sp):
            sp.dma_start(vec[:], a["vecs"]).then_inc(s_const, 16)
            sp.dma_start(identF[:], a["ident_f"]).then_inc(s_const, 16)
            sp.dma_start(pairs[:], a["pairs"]).then_inc(s_const, 16)
            sp.dma_start(identB[:], a["ident_b"]).then_inc(s_const, 16)
            for t in range(NB):
                sp.dma_start(xin[:, t, :], a["x"][0, P * t:P * t + P, :]).then_inc(s_x[t], 16)
            def load(n):
                if NRAW <= n < NU + NRAW:
                    sp.wait_ge(s_wL, n - NRAW + 1)
                elif n >= NU + NRAW:
                    c = n - NRAW - NU
                    sp.wait_ge(s_woH, c + 1)
                    sp.wait_ge((s_woLp, s_woLd)[c % 2], c // 2 + 1)
                if n == 0:
                    sp.dma_start(raw[:, 0, :, 0:72], a["w_ik"]).then_inc(s_raw[0], 16)
                elif n < NU:
                    sp.dma_start(raw[:, n % NRAW, :, :], a["w_units"][n - 1]).then_inc(s_raw[n % NRAW], 16)
                else:
                    sp.dma_start(raw[:, n % NRAW, :, :],
                                 a["w_out"][P * (n - NU):P * (n - NU) + P, :]
                                 .rearrange("p (k n) -> p k n", k=KT)).then_inc(s_raw[n % NRAW], 16)

            w_ada = a["w_ada"].rearrange("(k p) n -> k p n", p=P)
            for kt in range(KT):
                if kt >= 4:
                    sp.wait_ge(s_acc, kt - 3)
                sp.dma_start(wa[kt % 4][:], w_ada[kt, :, 0:2 * D]).then_inc(s_wa[kt % 4], 16)
                if kt in (3, 4):
                    load(kt - 3)

            for n in range(2, NRAW):
                load(n)
            sp.wait_ge(s_hL, KT - len(HL_POOL))
            sp.wait_ge(s_hLp, len(HL_POOL))
            sp.dma_start(posi[:], a["positions"][0:1, :].broadcast_to([P, S])).then_inc(s_pos, 16)

            def rope_out(sec):
                sp.wait_ge(s_evac, UNIT[(sec, NT - 1)] + 1)
                k = SECT[sec]
                for odd in range(2):
                    b = HD * odd
                    for (lo, n, dst, to) in ((0, 16, dx, 0), (0, 8, dp, 8), (8, 8, dp, 0)):
                        sp.dma_start(dst[k, odd::2, to:to + n, :].rearrange("t r s -> r t s"),
                                     T[sec][b + lo:b + lo + n, :, :]).then_inc(s_bounce, 16)
                sp.wait_ge(s_bounce, 16 * NBOUNCE * (k + 1) + 32 * k)
                sp.wait_ge(s_back, 16 if k == 0 else 16 + 32 * k)
                sp.dma_start(cx[:], dx[k].rearrange("h r s -> (h r) s")).then_inc(s_cx, 16)
                sp.dma_start(cs[:], dp[k].rearrange("h r s -> (h r) s")).then_inc(s_cx, 16)

            def rope_back(sec):
                k = SECT[sec]
                sp.wait_ge(s_rot, k + 2)
                sp.dma_start(dr[k].rearrange("h r s -> (h r) s"), cx[:]).then_inc(s_bounce, 32)
                sp.wait_ge(s_bounce, (16 * NBOUNCE + 32) * (k + 1))
                for odd in range(2):
                    sp.dma_start(T[sec][HD * odd:HD * odd + ROPE, :, :],
                                 dr[k, odd::2, :, :].rearrange("t r s -> r t s")).then_inc(s_back, 16)

            def spill(sec):
                for t in range(NT):
                    m = NT * SECT[sec] + t
                    sp.wait_ge(s_splH, m + 1)
                    sp.wait_ge(s_splL, m + 1)
                    for half, src in enumerate((hlH[m % 2], hlL[m % 2])):
                        if sec == "iq":
                            for odd in range(2):
                                sp.dma_start(iqs[HD * half:HD * half + HD, 2 * t + odd, :].bitcast(F32),
                                             src[HD * odd:HD * odd + HD, :].bitcast(F32)).then_inc(s_spill[m % 2], 16)
                        else:
                            sp.dma_start(dqk[("aq", "ak").index(sec), half, t], src[:].bitcast(F32)).then_inc(s_spill[m % 2], 32)

            for kind, n in SCHEDULE:
                if kind != "unit":
                    continue
                load(n + NRAW)
                if UNITS[n] == ("aq", 0):
                    sp.wait_ge(s_evac, 1)
                    sp.wait_ge(s_tab, 1)
                    sp.dma_start(cx[0:16, :], Tik[0:16, :]).then_inc(s_cx, 16)
                    sp.dma_start(cs[0:8, :], Tik[8:16, :]).then_inc(s_cx, 16)
                    sp.dma_start(cs[8:16, :], Tik[0:8, :]).then_inc(s_cx, 16)
                    sp.wait_ge(s_rot, 1)
                    sp.dma_start(Tik[0:16, :], cx[0:16, :]).then_inc(s_back, 16)
                if UNITS[n] == ("aq", 2):
                    sp.wait_ge(s_kiH, 1)
                    sp.dma_start(iks1[HD:P, :].bitcast(F32), iks1[0:HD, :].bitcast(F32)).then_inc(s_kidup, 16)
                    sp.wait_ge(s_kiL, 1)
                    sp.dma_start(iks2[HD:P, :].bitcast(F32), iks2[0:HD, :].bitcast(F32)).then_inc(s_kidup, 16)
                sec, t = UNITS[n]
                if sec in SECT and t == NT - 1:
                    rope_out(sec)
                if UNITS[n] in (("iq", 0), ("ak", 0), ("av", 2)):
                    rope_back({"iq": "aq", "ak": "iq", "av": "ak"}[sec])
                if UNITS[n] in (("iq", 2), ("ak", 2), ("cu", 0)):
                    spill({"iq": "aq", "ak": "iq", "cu": "ak"}[sec])

            sp.wait_ge(s_cvn, NT)
            sp.wait_ge(s_mask, NI)
            sp.dma_start(delta[:], a["delta"]).then_inc(s_delta, 16)
            for i in range(2):
                sp.wait_ge(s_spill[i], 16 * (4 * 2 + 4 * 4))
            for h in range(NH):
                if h >= 2:
                    sp.wait_ge(s_st, ST_AT[(h - 2, 1, NB - 1)] + 1)
                t, r = h // 2, rows(h)
                for i, dst in enumerate((qs, ks1, ks2)):
                    for half in range(2):
                        part = half if i == 0 else i - 1
                        sp.dma_start(dst[h % 2][HD * half:HD * half + HD, :].bitcast(F32),
                                     dqk[min(i, 1), part, t, r, :]).then_inc(s_stack[h % 2], 16)
                if h == 1:
                    for n in range(NU + NRAW, NU + KT):
                        load(n)
                    sp.wait_ge(s_woLp, KT // 2)
                    sp.wait_ge(s_woLd, KT // 2)
                    sp.wait_ge(s_woH, KT)
                if 1 <= h <= 4:
                    for kt in (2 * h - 2, 2 * h - 1):
                        if kt >= 2:
                            sp.wait_ge(s_gacc, kt - 1)
                        sp.dma_start(gw[:, kt % 2, :], w_ada[kt, :, 2 * D:3 * D]).then_inc(s_gw[kt % 2], 16)

            sp.wait_ge(s_pv, len(PV))
            sp.dma_start(normf[:], a["norm_f"].rearrange("(o n) -> o n", o=1).broadcast_to([P, D])).then_inc(s_nf, 16)
            sp.dma_start(bgate[:], a["b_gate"].rearrange("(o n) -> o n", o=1).broadcast_to([P, D])).then_inc(s_nf, 16)
            for b in range(2):
                sp.dma_start(xe[:, b, :], a["x"][0, P * b:P * b + P, :]).then_inc(s_xe[b], 16)
            for b in range(NB):
                sp.wait_ge(s_fin, b + 1)
                sp.dma_start(a["out"][0, P * b:P * b + P, :], oe[:, b % 2, :]).then_inc(s_out[b % 2], 16)
                if b + 2 < NB:
                    sp.wait_ge(s_res, b + 1)
                    sp.dma_start(xe[:, b % 2, :], a["x"][0, P * (b + 2):P * (b + 3), :]).then_inc(s_xe[b % 2], 16)
            for i in range(2):
                sp.wait_ge(s_out[i], 16 * (NB // 2))

        @block.tensor
        def _(pe):
            pe.wait_ge(s_const, 16 * 4)
            for kt in range(KT):
                if kt == 0:
                    pe.wait_ge(s_xn, NB)
                if kt >= 4:
                    pe.wait_ge(s_xt, kt - 3)
                for t in range(NB):
                    mm = pe.transpose(two(2 * (kt % 4))[:, P * t:P * t + P], xin[:, t, P * kt:P * kt + P], identF[:])
                mm.then_inc(s_xtp, 1)
            pe.wait_ge(s_acc, KT)
            pe.wait_ge(s_ones, 1)
            pe.wait_ge(s_xt, KT)
            for j in range(2 * KT):
                mm = pe.matmul(ps[:, 0, j:j + 1], acc[:, P * j:P * j + P], onesF[:], start=(j == 0), stop=True,
                               skip_group_check=True)
            mm.then_inc(s_modp, 1)

            def unit(n):
                m = 72 if n == 0 else P
                pe.wait_ge(s_wH, n + 1)
                pe.wait_ge(s_wL, n + 1)
                if n >= 2:
                    pe.wait_ge(s_evac, n - 1)
                if n == 0:
                    pe.wait_ge(s_h, 1)
                b, first = SCORES_IN.get(n, (0, 0))
                scored = 0
                for half in range(2):
                    out = ps[0:m, 2 * (n % 2) + half, :]
                    cols = slice(HALF * half, HALF * half + HALF)
                    for kt in range(KT):
                        if n == 0 and half == 0:
                            pe.wait_ge(s_hH, kt + 1)
                            if kt in HL_POOL:
                                pe.wait_ge(s_hLp, HL_POOL.index(kt) + 1)
                            else:
                                pe.wait_ge(s_hL, kt + 1 - sum(k < kt for k in HL_POOL))
                        pe.matmul(out, wH[:, n % 2, kt, 0:m], hH[:, kt, cols], start=(kt == 0), stop=False)
                        pe.matmul(out, wH[:, n % 2, kt, 0:m], hL[:, kt, cols], start=False, stop=False)
                        mm = pe.matmul(out, wL[:, n % 2, kt, 0:m], hH[:, kt, cols], start=False, stop=(kt == KT - 1))
                        at_step = KT * half + kt + 1
                        while b and at_step > first and scored * (2 * KT - first) < 2 * NIH * (at_step - first):
                            index_scores(b + scored // NIH, scored % NIH)
                            scored += 1
                mm.then_inc(s_unit, 1)

            def index_scores(i, h):
                n = (i + 1) * P
                u = NIH * (i - 2) + h
                if u == 0:
                    pe.wait_ge(s_kidup, 32)
                    pe.wait_ge(s_spill[0], 64 * 4)
                    pe.wait_ge(s_spill[1], 64 * 4)
                    pe.wait_ge(s_iw, 1)
                if u >= 2:
                    pe.wait_ge(s_relu, u - 1)
                dst = two(4 + 2 * (u % 2))
                for o in range(0, n, HALF):
                    e = min(n, o + HALF)
                    pe.matmul(dst[:, o:e], iqs[:, h, P * i:P * i + P], iks1[:, o:e], start=True, stop=False)
                    mm = pe.matmul(dst[:, o:e], iqs[:, h, P * i:P * i + P], iks2[:, o:e], start=False, stop=True)
                mm.then_inc(s_idx, 1)

            for kind, n in SCHEDULE:
                if kind == "unit":
                    unit(n)
                elif kind == "iwt":
                    pe.wait_ge(s_evac, 1)
                    for b in range(NB):
                        mm = pe.transpose(ps[:, 4, NIH * b:NIH * b + NIH], Tik[64:72, P * b:P * b + P], identF[64:72, 64:72])
                    mm.then_inc(s_iwt, 1)
                elif kind == "vt":
                    pe.wait_ge(s_evac, UNIT[("av", n)] + 1)
                    if n == 0:
                        pe.wait_ge(s_relu, 8 * len(IDX_BLOCKS))
                    if n >= 2:
                        pe.wait_ge(s_v, n - 1)
                    for b in range(NB):
                        mm = pe.transpose(two(4 + 2 * (n % 2))[:, P * b:P * b + P], vst[:, n % 2, P * b:P * b + P], identF[:])
                    mm.then_inc(s_vt, 1)
                elif kind == "cn":
                    pe.wait_ge(s_cvq, n + 1)
                    if n == 0:
                        pe.wait_ge(s_v, NT)
                    else:
                        pe.wait_ge(s_cvd, n)
                    for half in range(2):
                        mm = pe.matmul(ps[:, 4 + half, :], pairs[:], conv0[:, HALF * half:HALF * half + HALF], start=True, stop=True)
                    mm.then_inc(s_cvp, 1)

            def logits(h):
                pe.wait_ge(s_stack[h % 2], 96 * (h // 2 + 1))
                for i in range(NB):
                    u = NB * h + i
                    n = (i + 1) * P
                    if u == 0:
                        pe.wait_ge(s_evac, NU)
                    if u >= 2:
                        pe.wait_ge(s_mx, u - 1)
                    dst = two(2 * (u % 2))
                    for o in range(0, n, HALF):
                        e = min(n, o + HALF)
                        pe.matmul(dst[:, o:e], qs[h % 2][:, P * i:P * i + P], ks1[h % 2][:, o:e], start=True, stop=False)
                        mm = pe.matmul(dst[:, o:e], qs[h % 2][:, P * i:P * i + P], ks2[h % 2][:, o:e], start=False, stop=True)
                    mm.then_inc(s_lg, 1)

            def st_slot(u):
                if u == 0:
                    pe.wait_ge(s_cvd, NT)
                if u >= 2:
                    hh, sb, j, _ = ST[u - 2]
                    if sb == MAXIMA:
                        pe.wait_ge(s_mrow, hh + 1)
                    elif sb == SUMS:
                        pe.wait_ge(s_yln, 2 * hh + j + 1)
                    else:
                        pe.wait_ge(s_exp, PV_AT[(hh, sb, j)] + 1)
                return 4 + u % 2

            def maxima(h):
                bank = st_slot(ST_AT[(h, -1, 0)])
                pe.wait_ge(s_mp, h + 1)
                pe.transpose(ps[0:16, bank, :].bitcast(BF16)[:, 0:P], mparts[:], identB[:]).then_inc(s_mt, 1)

            def scores_t(u):
                h, sb, j, c = ST[u]
                if (sb, j) == (0, 0):
                    pe.wait_ge(s_mrow, h + 1)
                bank = st_slot(u)
                out = ps[:, bank, P * c:HALF]
                cols = slice(HALF * sb + P * c, HALF * sb + HALF)
                keys = slice(P * j, P * j + P)
                pe.matmul(out, ks1[h % 2][:, keys], qs[h % 2][:, cols], start=True, stop=False, skip_group_check=True)
                pe.matmul(out, ks2[h % 2][:, keys], qs[h % 2][:, cols], start=False, stop=False, skip_group_check=True)
                for b in range(c, 4):
                    i = 4 * sb + b
                    if i >= 2 or i == j:
                        pe.matmul(ps[:, bank, P * b:P * b + P], bias_of(i)[:, keys], identB[:], start=False, stop=False,
                                  skip_group_check=True)
                pe.matmul(out, onesB[:], mrow[:, 4 * sb + c:4 * sb + 4, :].rearrange("p b n -> p (b n)"), start=False,
                          stop=True, skip_group_check=True).then_inc(s_st, 1)

            def values(k):
                h, sb, j, c = PV[k]
                pe.wait_ge(s_exp, k + 1)
                if j == 0 and 2 * h + sb >= 2:
                    pe.wait_ge(s_o, 2 * h + sb - 1)
                w = V[:, j, h // 2, HD * (h % 2):HD * (h % 2) + P]
                pe.matmul(ps[:, 6 + sb, P * c:HALF], w, prob[:, k % 4, P * c:HALF], start=(j == 0),
                          stop=(j == 4 * sb + 3), skip_group_check=True).then_inc(s_pv, 1)

            def group_sums(t):
                pe.wait_ge(s_ysq, t + 1)
                for half in range(2):
                    bank = st_slot(ST_AT[(t, SUMS, half)])
                    pe.matmul(ps[:, bank, :], pairs[:], ysq[:, HALF * half:HALF * half + HALF], start=True,
                              stop=True).then_inc(s_yss, 1)

            pe.wait_ge(s_vones, 5)
            pe.wait_ge(s_mask, len(IDX_BLOCKS))
            logits(0)
            maxima(0)
            for h in range(NH):
                first = PV_AT[(h, 0, 0)]
                count = len(chunks(0)) + len(chunks(1))
                for x in range(count):
                    scores_t(ST_AT[PV[first + x][:3]])
                    if x >= 1:
                        values(first + x - 1)
                if h in SUMS_AFTER and h < NH - 1:
                    group_sums(SUMS_AFTER[h])
                if h + 1 < NH:
                    logits(h + 1)
                values(first + count - 1)
                if h + 1 < NH:
                    maxima(h + 1)
            pe.wait_ge(s_gacc, KT)
            pe.wait_ge(s_onesq, 1)
            pe.wait_ge(s_mx, NB * NH)
            for half in range(2):
                mm = pe.matmul(ps[:, 2 + half, :], onesq[:], gate[:, HALF * half:HALF * half + HALF], start=True, stop=True)
            mm.then_inc(s_gp, 1)
            group_sums(NT - 1)

            pe.wait_ge(s_woLp, KT // 2)
            pe.wait_ge(s_woLd, KT // 2)
            pe.wait_ge(s_woH, KT)
            for b in range(NB):
                if b == 1:
                    pe.wait_ge(s_gate, 1)
                if b >= 2:
                    pe.wait_ge(s_og, b - 1)
                for part in range(2):
                    pe.wait_ge(s_yH, 2 * b + part + 1)
                    pe.wait_ge(s_yL, 2 * b + part + 1)
                    for half in range(2):
                        out = ps[:, 2 * (b % 2) + half, :]
                        cols = slice(HALF * half, HALF * half + HALF)
                        for ct in range(NT * part, NT * part + NT):
                            pe.matmul(out, yH[b % 2][:, ct, :], hH[:, ct, cols], start=(ct == 0), stop=False)
                            pe.matmul(out, yH[b % 2][:, ct, :], hL[:, ct, cols], start=False, stop=False)
                            mm = pe.matmul(out, yL[b % 2][:, ct, :], hH[:, ct, cols], start=False, stop=(ct == KT - 1))
                mm.then_inc(s_op, 1)

        @block.scalar
        def _(act):
            A = nc.scalar.activation
            act.wait_ge(s_const, 16 * 4)
            A(csilu, vec[:, V_C:V_C + KT], ACT.Silu).then_inc(s_csilu, 1)
            for t in range(NB):
                act.wait_ge(s_x[t], 16)
                if t >= 4:
                    act.wait_ge(s_sumsq, t - 3)
                A(two(2 * (t % 4)), xin[:, t, :], ACT.Square, accum_out=sumsq[:, t:t + 1]).then_inc(s_sumsq, 1)
            act.wait_ge(s_var, 1)
            A(rstd, sumsq, ACT.Sqrt).then_inc(s_std, 1)
            for kt in range(KT):
                act.wait_ge(s_xtp, kt + 1)
                A(xT[:, kt, :], two(2 * (kt % 4)), ACT.Copy).then_inc(s_xt, 1)

            def split_high(n):
                act.wait_ge(s_raw[n % NRAW], 16 * (n // NRAW + 1))
                if n < NU:
                    if n >= 2:
                        act.wait_ge(s_unit, n - 1)
                    m = 72 if n == 0 else P
                    A(wH[:, n % 2, :, 0:m], raw[:, n % NRAW, :, 0:m], ACT.Copy).then_inc(s_wH, 1)
                else:
                    act.wait_ge(s_unit, NU)
                    A(hH[:, n - NU, :], raw[:, n % NRAW, :, :].rearrange("p k n -> p (k n)"), ACT.Copy).then_inc(s_woH, 1)

            split_high(0)
            split_high(1)
            for kt in range(KT):
                act.wait_ge(s_h, kt + 1)
                A(hH[:, kt, :], xT[:, kt, :], ACT.Copy).then_inc(s_hH, 1)
            act.wait_ge(s_red, 1)
            A(tabS[:], ang[:], ACT.Sin).then_inc(s_trig, 1)
            A(turns[:], ang[:], ACT.Abs).then_inc(own_act, 1)
            act.wait_ge(s_red, 2)
            A(tabC[:], turns[:], ACT.Sin).then_inc(s_trig, 1)

            def evacuate(n):
                sec, t = UNITS[n]
                act.wait_ge(s_unit, n + 1)
                src = two(2 * (n % 2))
                if sec == "ik":
                    A(Tik[0:72, :], src[0:72, :], ACT.Copy).then_inc(s_evac, 1)
                elif sec in SECT:
                    if sec == "ak" and t == 0:
                        act.wait_ge(s_splL, NT)
                    A(T[sec][:, t, :], src, ACT.Copy).then_inc(s_evac, 1)
                elif sec == "av":
                    if t == 0:
                        act.wait_ge(s_idx, NIH * len(IDX_BLOCKS))
                    if t >= 2:
                        act.wait_ge(s_vt, t - 1)
                    A(vst[:, t % 2, :], src, ACT.Copy).then_inc(s_evac, 1)
                elif sec == "cc":
                    if t >= 1:
                        act.wait_ge(s_cvs, t)
                    A(convc[:], src, ACT.Copy).then_inc(s_evac, 1)
                elif sec == "cu":
                    A(convu[:], src, ACT.Copy).then_inc(s_evac, 1)
                elif sec == "cb":
                    if t == 0:
                        act.wait_ge(s_splL, 3 * NT)
                    else:
                        act.wait_ge(s_cvn, t)
                    A(convb[:], src, ACT.Copy).then_inc(s_evac, 1)
                elif sec == "cz":
                    if t == 0:
                        act.wait_ge(s_spill[0], 16 * 24)
                        act.wait_ge(s_spill[1], 16 * 24)
                    A(yconv[:, t, :], src, ACT.Silu).then_inc(s_evac, 1)
                elif sec == "az":
                    A(azs[:, t, :], src, ACT.Silu).then_inc(s_evac, 1)

            def taps(t):
                act.wait_ge(s_cvs, t + 1)
                A(conv0[:], convs[:, 2:2 + S], ACT.Identity, bias=vec[:, V_CB + t:V_CB + t + 1],
                  scale=vec[:, V_CW + 8 + t:V_CW + 9 + t]).then_inc(s_cvt, 1)
                A(conv1[:], convs[:, 1:1 + S], ACT.Copy, scale=vec[:, V_CW + 4 + t:V_CW + 5 + t]).then_inc(s_cvt, 1)
                act.wait_ge(s_cvy, 2 * t + 1)
                A(conv1[:], convs[:, 0:S], ACT.Copy, scale=vec[:, V_CW + t:V_CW + 1 + t]).then_inc(s_cvt, 1)

            for kind, n in SCHEDULE:
                if kind == "unit":
                    evacuate(n)
                    if n + 2 < NU:
                        split_high(n + 2)
                    sec, t = UNITS[n]
                    if sec == "cb":
                        taps(t)
                    if sec == "cz":
                        act.wait_ge(s_cvy, 2 * t + 2)
                        A(conv0[:], convb[:], ACT.Square).then_inc(s_cvq, 1)
                    if UNITS[n] == ("aq", 1):
                        act.wait_ge(s_back, 16)
                        A(iks1[0:HD, :], Tik[0:HD, :], ACT.Copy).then_inc(s_kiH, 1)
                elif kind == "idx":
                    for h in range(NIH):
                        u = NIH * (n - 2) + h
                        act.wait_ge(s_idx, u + 1)
                        if u >= 2:
                            act.wait_ge(s_score, u - 1)
                        w = (n + 1) * P
                        A(relu[:, u % 2, 0:w], two(4 + 2 * (u % 2))[:, 0:w], ACT.Relu, scale=wabs[:, n, h:h + 1]).then_inc(s_relu, 1)
                elif kind == "vt":
                    act.wait_ge(s_vt, n + 1)
                    src = two(4 + 2 * (n % 2)).rearrange("p (b g d) -> p b g d", b=NB, g=2)
                    for g in range(2):
                        mm = A(V[:, :, n, 2 * HD * g:2 * HD * g + HD], src[:, :, g, :], ACT.Copy)
                    mm.then_inc(s_v, 1)
                elif kind == "cn":
                    act.wait_ge(s_cvp, n + 1)
                    A(conv1[:], two(4), ACT.Ln, scale=1.0 / HD, bias=vec[:, V_EPS:V_EPS + 1]).then_inc(s_cvd, 1)
                    act.wait_ge(s_cvd, n + 1)
                    A(conv1[:], conv1[:], ACT.Exp, scale=-0.5).then_inc(s_cvr, 1)
                if (kind, n) in SPLITS:
                    sec = SPLITS[(kind, n)]
                    for t in range(NT):
                        m = NT * SECT[sec] + t
                        if t == 0:
                            act.wait_ge(s_back, 16 + 32 * (SECT[sec] + 1))
                        if m >= 2:
                            act.wait_ge(s_spill[m % 2], 64 * (m // 2))
                        A(hlH[m % 2][:], T[sec][:, t, :], ACT.Copy).then_inc(s_splH, 1)

            for n in range(NU, NU + KT):
                split_high(n)

            def exps(h):
                for sb in range(2):
                    for j, c in chunks(sb):
                        k = PV_AT[(h, sb, j)]
                        act.wait_ge(s_st, k + 1)
                        if k == 0:
                            act.wait_ge(s_vt, NT)
                        if k >= 4:
                            act.wait_ge(s_pv, k - 3)
                        A(prob[:, k % 4, P * c:HALF], ps[:, 4 + ST_AT[(h, sb, j)] % 2, P * c:HALF], ACT.Exp,
                          scale=ATT_SCALE).then_inc(s_exp, 1)

            def pair_rstd(t):
                for half in range(2):
                    act.wait_ge(s_yss, 2 * t + half + 1)
                    z = ysq[:, HALF * half:HALF * half + HALF]
                    A(z, ps[:, 4 + ST_AT[(t, SUMS, half)] % 2, :], ACT.Ln, scale=1.0 / HD,
                      bias=vec[:, V_EPS:V_EPS + 1]).then_inc(s_yln, 1)
                    act.wait_ge(s_yln, 2 * t + half + 1)
                    A(z, z, ACT.Exp, scale=-0.5).then_inc(s_yrs, 1)

            def high(b, part):
                if b >= 2:
                    act.wait_ge(s_op, b - 1)
                if part:
                    act.wait_ge(s_ya, NT)
                A(yH[b % 2][:, NT * part:NT * part + NT, :], (yconv, ya)[part][:, :, P * b:P * b + P], ACT.Copy).then_inc(s_yH, 1)

            for h in range(NH):
                exps(h)
                if h == NH - 1:
                    act.wait_ge(s_pv, len(PV))
                    high(0, 0)
                if h in SUMS_AFTER:
                    pair_rstd(SUMS_AFTER[h])
            high(0, 1)
            high(1, 0)
            high(1, 1)
            for b in range(NB):
                if b + 2 < NB:
                    high(b + 2, 0)
                    high(b + 2, 1)
                act.wait_ge(s_res, b + 1)
                if b >= 2:
                    act.wait_ge(s_out[b % 2], 16 * (b // 2))
                A(oe[:, b % 2, :], te[:, b % 2, :], ACT.Square, accum_out=fin[:, b:b + 1]).then_inc(s_fsq, 1)
                act.wait_ge(s_fv, b + 1)
                A(finr[:, b:b + 1], fin[:, b:b + 1], ACT.Sqrt).then_inc(s_fs, 1)

        @block.vector
        def _(dve):
            v = nc.vector
            chain = [0]

            def link(ins):
                chain[0] += 1
                ins.then_inc(own_dve, 1)
                dve.wait_ge(own_dve, chain[0])

            v.memset(onesF[:], 1.0).then_inc(s_ones, 1)
            for r in range(ROUND):
                v.memset(ramp[:, r:r + 1], float(r)).then_inc(s_ones, 1)
            dve.wait_ge(s_sumsq, NB)
            v.tensor_scalar(sumsq, sumsq, 1.0 / D, EPS, ALU.mult, ALU.add).then_inc(s_var, 1)
            dve.wait_ge(s_std, 1)
            link(v.reciprocal(rstd, rstd))
            for t in range(NB):
                v.tensor_scalar(xin[:, t, :], xin[:, t, :], rstd[:, t:t + 1], None, ALU.mult).then_inc(s_xn, 1)
            dve.wait_ge(s_csilu, 1)
            for kt in range(KT):
                dve.wait_ge(s_wa[kt % 4], 16 * (kt // 4 + 1))
                if kt == 0:
                    v.tensor_scalar(acc[:], wa[0][:], csilu[:, 0:1], None, ALU.mult).then_inc(s_acc, 1)
                else:
                    dve.wait_ge(s_acc, kt)
                    v.scalar_tensor_tensor(acc[:], wa[kt % 4][:], csilu[:, kt:kt + 1], acc[:], ALU.mult, ALU.add).then_inc(s_acc, 1)
            dve.wait_ge(s_modp, 1)
            v.tensor_tensor(shift, ps[:, 0, 0:KT], vec[:, V_BSH:V_BSH + KT], ALU.add)
            link(v.tensor_tensor(amp, ps[:, 0, KT:2 * KT], vec[:, V_BSC:V_BSC + KT], ALU.add))
            link(v.scalar_tensor_tensor(amp, amp, 1.0, vec[:, V_NORM:V_NORM + KT], ALU.add, ALU.mult))
            for kt in range(KT + 1):
                if kt < KT:
                    dve.wait_ge(s_xt, kt + 1)
                    v.tensor_scalar(xT[:, kt, :], xT[:, kt, :], amp[:, kt:kt + 1], shift[:, kt:kt + 1], ALU.mult, ALU.add).then_inc(s_h, 1)
                if kt >= 1 and kt - 1 not in HL_POOL:
                    low_h(v, dve, kt - 1, s_hL)

            dve.wait_ge(s_pos, 16)
            link(v.tensor_copy(ang[:], posi[:]))
            link(v.tensor_scalar(ang[:], ang[:], vec[:, V_FREQ:V_FREQ + 1], None, ALU.mult))
            link(v.tensor_scalar(turns[:], ang[:], 1.0 / (2 * np.pi), MAGIC, ALU.mult, ALU.add))
            link(v.tensor_scalar(turns[:], turns[:], MAGIC, None, ALU.subtract))
            for part in two_pi_parts():
                link(v.scalar_tensor_tensor(ang[:], turns[:], -part, ang[:], ALU.mult, ALU.add))
            v.tensor_scalar(ang[:], ang[:], PI, -PI, ALU.min, ALU.max).then_inc(s_red, 1)
            dve.wait_ge(own_act, 1)
            v.tensor_scalar(turns[:], turns[:], -1.0, float(np.pi / 2), ALU.mult, ALU.add).then_inc(s_red, 1)
            dve.wait_ge(s_trig, 2)
            v.tensor_scalar(tabS[:], tabS[:], vec[:, V_SIGN:V_SIGN + 1], None, ALU.mult).then_inc(s_tab, 1)
            dve.wait_ge(s_tab, 1)

            def rotate(k, n, count):
                dve.wait_ge(s_cx, count)
                v.tensor_tensor(cx[0:n, :], cx[0:n, :], tabC[0:n, :], ALU.mult)
                link(v.tensor_tensor(cs[0:n, :], cs[0:n, :], tabS[0:n, :], ALU.mult))
                v.tensor_tensor(cx[0:n, :], cx[0:n, :], cs[0:n, :], ALU.add).then_inc(s_rot, 1)

            rotate(0, ROPE, 48)
            dve.wait_ge(s_iwt, 1)
            iwp = ps[:, 4, 0:NB * NIH]
            wf = wabs[:].rearrange("p b h -> p (b h)")
            wg = wsgn[:].rearrange("p b h -> p (b h)")
            link(v.tensor_scalar(wg, iwp, 0.0, 2.0, ALU.is_ge, ALU.mult))
            link(v.tensor_scalar(wg, wg, 1.0, None, ALU.subtract))
            v.scalar_tensor_tensor(wf, iwp, IDX_SCALE, wg, ALU.mult, ALU.mult).then_inc(s_iw, 1)
            dve.wait_ge(s_kiH, 1)
            v.tensor_tensor(iks2[0:HD, :], Tik[0:HD, :], iks1[0:HD, :].bitcast(F32), ALU.subtract).then_inc(s_kiL, 1)
            rotate(1, P, 48 + 32)
            dve.wait_ge(s_kiL, 1)
            for t in range(NT):
                section_low(v, dve, "aq", t)
            rotate(2, P, 48 + 64)
            for t in range(NT):
                section_low(v, dve, "iq", t)
            dve.wait_ge(s_iw, 1)
            dve.wait_ge(s_splL, 2 * NT)
            for i in IDX_BLOCKS:
                n = (i + 1) * P
                for h in range(NIH):
                    u = NIH * (i - 2) + h
                    dve.wait_ge(s_relu, u + 1)
                    if h == 0:
                        v.tensor_scalar(score_of(i), relu[:, u % 2, 0:n], wsgn[:, i, 0:1], None, ALU.mult).then_inc(s_score, 1)
                    else:
                        dve.wait_ge(s_score, u)
                        v.scalar_tensor_tensor(score_of(i), relu[:, u % 2, 0:n], wsgn[:, i, h:h + 1], score_of(i),
                                               ALU.mult, ALU.add).then_inc(s_score, 1)
                b = i - IDX_BLOCKS[0]
                dve.wait_ge(s_score, NIH * (b + 1))
                v.tensor_reduce(lo[:, b:b + 1], score_of(i), mybir.AxisListType.X, ALU.min).then_inc(s_range, 1)
                v.tensor_reduce(step[:, b:b + 1], score_of(i), mybir.AxisListType.X, ALU.max).then_inc(s_range, 1)

            def find_threshold():
                dve.wait_ge(s_range, 2 * NI)
                link(v.tensor_tensor(step, step, lo, ALU.subtract))
                link(v.tensor_scalar(step, step, 0.5, None, ALU.mult))
                link(v.memset(hi, -TAKEN))
                dve.wait_ge(s_caus, NI)
                with dve.Fori(0, HALVINGS):
                    v.tensor_tensor(cand, lo, step, ALU.add).then_inc(s_halve, 1)
                    dve.wait_ge(s_halve, 1)
                    for b, i in enumerate(IDX_BLOCKS):
                        if b:
                            dve.wait_ge(s_halve, b + 1)
                        v.tensor_scalar(above[:, 0:(i + 1) * P], score_of(i), cand[:, b:b + 1], None, ALU.is_ge, ALU.add,
                                        accum_out=count[:, b:b + 1]).then_inc(s_halve, 1)
                    dve.wait_ge(s_halve, NI + 1)
                    v.tensor_scalar(good, count, float(TOPK), None, ALU.is_ge).then_inc(s_halve, 1)
                    dve.wait_ge(s_halve, NI + 2)
                    v.tensor_tensor(count, good, step, ALU.mult).then_inc(s_halve, 1)
                    v.scalar_tensor_tensor(good, good, -TAKEN, cand, ALU.mult, ALU.add).then_inc(s_halve, 1)
                    dve.wait_ge(s_halve, NI + 4)
                    v.tensor_tensor(lo, lo, count, ALU.add).then_inc(s_halve, 1)
                    v.tensor_tensor(hi, hi, good, ALU.min).then_inc(s_halve, 1)
                    v.tensor_scalar(step, step, 0.5, None, ALU.mult).then_inc(s_halve, 1)
                    dve.wait_ge(s_halve, NI + 7)
                    dve.sem_clear(s_halve)

            def take_above():
                for b, i in enumerate(IDX_BLOCKS):
                    n = (i + 1) * P
                    if b:
                        dve.wait_ge(s_count, 2 * b)
                    v.tensor_scalar(above[:, 0:n], score_of(i), hi[:, b:b + 1], None, ALU.is_ge, ALU.add,
                                    accum_out=count[:, b:b + 1]).then_inc(s_count, 1)
                    dve.wait_ge(s_count, 2 * b + 1)
                    v.scalar_tensor_tensor(score_of(i), above[:, 0:n], TAKEN, score_of(i), ALU.mult, ALU.add).then_inc(s_count, 1)
                dve.wait_ge(s_count, 2 * NI)
                v.tensor_scalar(need, count, -1.0, float(TOPK), ALU.mult, ALU.add).then_inc(s_need, 1)
                dve.wait_ge(s_most, 1)
                link(v.tensor_scalar(most, most, 1.0 / ROUND, 0.5 - 0.5 / ROUND, ALU.mult, ALU.add))
                link(v.tensor_scalar(most, most, MAGIC, None, ALU.add))
                link(v.tensor_scalar(most, most, MAGIC, None, ALU.subtract))
                link(v.tensor_copy(rounds[:], most))

            def top_keys(i):
                sc = score_of(i)
                b = i - IDX_BLOCKS[0]
                mine = need[:, b:b + 1]
                with dve.Fori(0, dve.value_load(rounds[0:1, b:b + 1], min_val=1, max_val=TOPK // ROUND)):
                    v.max(m8[:], sc).then_inc(s_round, 1)
                    v.tensor_scalar(limit, ramp, mine, 2.0, ALU.is_lt, ALU.mult).then_inc(s_round, 1)
                    dve.wait_ge(s_round, 2)
                    v.tensor_scalar(limit, limit, 1.0, -TAKEN, ALU.subtract, ALU.mult).then_inc(s_round, 1)
                    v.tensor_scalar(mine, mine, float(ROUND), None, ALU.subtract).then_inc(s_round, 1)
                    dve.wait_ge(s_round, 4)
                    v.tensor_tensor(m8[:], m8[:], limit, ALU.min).then_inc(s_round, 1)
                    dve.wait_ge(s_round, 5)
                    v.match_replace(sc, m8[:], sc, TAKEN).then_inc(s_round, 1)
                    dve.wait_ge(s_round, 6)
                    dve.sem_clear(s_round)
                v.tensor_scalar(bias_of(i), sc, TAKEN, -BIG, ALU.not_equal, ALU.mult).then_inc(s_mask, 1)

            rotate(3, P, 48 + 96)
            dve.wait_ge(s_ones, 1 + ROUND)
            find_threshold()
            take_above()
            for i in IDX_BLOCKS:
                top_keys(i)
            for c in range(1, KT, 2):
                out_low(v, dve, c, s_woLd)
            dve.wait_ge(s_mask, len(IDX_BLOCKS))
            dve.wait_ge(s_vones, 5)

            def row_max(h):
                for i in range(NB):
                    u = NB * h + i
                    dve.wait_ge(s_lg, u + 1)
                    src = two(2 * (u % 2))[:, 0:(i + 1) * P]
                    v.tensor_tensor_reduce(src, src, bias_of(i), 1.0, -3.0e38, ALU.add, ALU.max, mx[:, i:i + 1]).then_inc(s_mx, 1)
                dve.wait_ge(s_mx, NB * (h + 1))
                if h >= 1:
                    dve.wait_ge(s_mt, h)
                link(v.tensor_scalar(mparts[:, 0:NB], mx[:], -1.0, None, ALU.mult))
                v.scalar_tensor_tensor(mparts[:, NB:2 * NB], mx[:], -1.0, mparts[:, 0:NB], ALU.mult, ALU.subtract).then_inc(s_mp, 1)

            def max_rows(h):
                dve.wait_ge(s_mt, h + 1)
                if h == 0:
                    dve.wait_ge(s_delta, 16)
                else:
                    dve.wait_ge(s_st, PV_AT[(h - 1, 1, NB - 1)] + 1)
                src = ps[0:16, 4 + ST_AT[(h, -1, 0)] % 2, :].bitcast(BF16)[:, 0:P]
                v.tensor_tensor(mrow[:], src.rearrange("p (o n) -> p o n", o=1).broadcast_to([16, NB, P]), delta[:],
                                ALU.mult).then_inc(s_mrow, 1)

            def head_out(h, sb):
                dve.wait_ge(s_pv, PV_AT[(h, sb, 4 * sb + 3)] + 1)
                r, d = rows(h), rows(h + 1)
                if 2 * h + sb:
                    dve.wait_ge(s_o, 2 * h + sb)
                link(v.reciprocal(rden[r, :], ps[d, 6 + sb, :]))
                v.tensor_tensor(ya[r, h // 2, HALF * sb:HALF * sb + HALF], ps[r, 6 + sb, :], rden[r, :], ALU.mult).then_inc(s_o, 1)

            def gate_sum(kt):
                dve.wait_ge(s_gw[kt % 2], 16 * (kt // 2 + 1))
                if kt == 0:
                    v.tensor_scalar(gate[:], gw[:, 0, :], csilu[:, 0:1], None, ALU.mult).then_inc(s_gacc, 1)
                else:
                    dve.wait_ge(s_gacc, kt)
                    v.scalar_tensor_tensor(gate[:], gw[:, kt % 2, :], csilu[:, kt:kt + 1], gate[:], ALU.mult, ALU.add).then_inc(s_gacc, 1)

            def pair_gate(t):
                dve.wait_ge(s_yn, t + 1)
                v.scalar_tensor_tensor(ya[:, t, :], ya[:, t, :], vec[:, V_GA + t:V_GA + t + 1], azs[:, t, :],
                                       ALU.mult, ALU.mult).then_inc(s_ya, 1)

            def low_y(b, part):
                dve.wait_ge(s_yH, 2 * b + part + 1)
                k = slice(NT * part, NT * part + NT)
                v.tensor_tensor(yL[b % 2][:, k, :], (yconv, ya)[part][:, :, P * b:P * b + P],
                                yH[b % 2][:, k, :].bitcast(F32), ALU.subtract).then_inc(s_yL, 1)

            row_max(0)
            max_rows(0)
            dve.wait_ge(s_woLp, KT // 2)
            dve.wait_ge(s_woH, KT)
            for h in range(NH):
                head_out(h, 0)
                if h + 1 < NH:
                    row_max(h + 1)
                head_out(h, 1)
                if 1 <= h <= 4:
                    gate_sum(2 * h - 2)
                    gate_sum(2 * h - 1)
                if h + 1 < NH:
                    max_rows(h + 1)
                if h in (3, 5, 7):
                    pair_gate(h // 2 - 1)
            low_y(0, 0)
            dve.wait_ge(s_gp, 1)
            dve.wait_ge(s_nf, 32)
            v.tensor_tensor(gate[:], two(2), bgate[:], ALU.add).then_inc(s_gate, 1)
            pair_gate(NT - 1)
            low_y(0, 1)
            low_y(1, 0)
            low_y(1, 1)
            dve.wait_ge(s_gate, 1)
            for b in range(NB):
                dve.wait_ge(s_op, b + 1)
                if b >= 2:
                    dve.wait_ge(s_fin, b - 1)
                v.tensor_tensor(te[:, b % 2, :], two(2 * (b % 2)), gate[:], ALU.mult).then_inc(s_og, 1)
                if b + 2 < NB:
                    low_y(b + 2, 0)
                    low_y(b + 2, 1)
                dve.wait_ge(s_fsq, b + 1)
                v.tensor_scalar(fin[:, b:b + 1], fin[:, b:b + 1], 1.0 / D, EPS, ALU.mult, ALU.add).then_inc(s_fv, 1)
                dve.wait_ge(s_fs, b + 1)
                link(v.reciprocal(finr[:, b:b + 1], finr[:, b:b + 1]))
                if b >= 2:
                    dve.wait_ge(s_out[b % 2], 16 * (b // 2))
                v.scalar_tensor_tensor(oe[:, b % 2, :], te[:, b % 2, :], finr[:, b:b + 1], normf[:], ALU.mult, ALU.mult).then_inc(s_fin, 1)

        @block.gpsimd
        def _(pool):
            g = nc.gpsimd
            g.memset(onesB[:], 1.0).then_inc(s_vones, 1)

            def split_low(n):
                m = 72 if n == 0 else P
                pool.wait_ge(s_wH, n + 1)
                g.tensor_tensor(wL[:, n % 2, :, 0:m], raw[:, n % NRAW, :, 0:m], wH[:, n % 2, :, 0:m].bitcast(F32),
                                ALU.subtract).then_inc(s_wL, 1)

            split_low(0)
            split_low(1)
            for kt in HL_POOL:
                low_h(g, pool, kt, s_hLp)
            for kind, n in SCHEDULE:
                if kind == "unit":
                    sec, t = UNITS[n]
                    if sec != "cb" and n + 2 < NU:
                        split_low(n + 2)
                    if sec == "cb":
                        pool.wait_ge(s_evac, UNIT[("cu", t)] + 1)
                        if t == 0:
                            pool.wait_ge(s_splL, 3 * NT)
                            g.memset(convs[:, 0:2], 0.0).then_inc(s_pad, 1)
                        g.tensor_tensor(convs[:, 2:2 + S], convc[:], convu[:], ALU.mult).then_inc(s_cvs, 1)
                        split_low(n + 2)
                        pool.wait_ge(s_cvt, 3 * t + 2)
                        g.tensor_tensor(conv0[:], conv0[:], conv1[:], ALU.add).then_inc(s_cvy, 1)
                        pool.wait_ge(s_cvt, 3 * t + 3)
                        pool.wait_ge(s_cvy, 2 * t + 1)
                        g.tensor_tensor(conv0[:], conv0[:], conv1[:], ALU.add).then_inc(own_pool, 1)
                        pool.wait_ge(own_pool, 3 * t + 1)
                        pool.wait_ge(s_evac, n + 1)
                        g.tensor_tensor(convb[:], convb[:], conv0[:], ALU.mult).then_inc(s_cvy, 1)
                elif kind == "idx":
                    pool.wait_ge(s_score, NIH * (n - 1))
                    pool.wait_ge(s_range, 2 * (n - 1))
                    d = score_of(n)[:, P * n:P * n + P]
                    g.affine_select(out=d, in_=d, compare_op=ALU.is_ge, fill=FUTURE, base=0, pattern=[[-1, P]],
                                    channel_multiplier=1).then_inc(s_caus, 1)
                elif kind == "cn":
                    pool.wait_ge(s_cvr, n + 1)
                    pool.wait_ge(s_cvy, 2 * n + 2)
                    g.tensor_tensor(convb[:], convb[:], conv1[:], ALU.mult).then_inc(own_pool, 1)
                    pool.wait_ge(own_pool, 3 * n + 2)
                    g.tensor_scalar(convb[:], convb[:], vec[:, V_GC + n:V_GC + n + 1], None, ALU.mult).then_inc(own_pool, 1)
                    pool.wait_ge(own_pool, 3 * n + 3)
                    pool.wait_ge(s_evac, UNIT[("cz", n)] + 1)
                    g.tensor_tensor(yconv[:, n, :], yconv[:, n, :], convb[:], ALU.mult).then_inc(s_cvn, 1)
                if (kind, n) == ("unit", 5):
                    g.memset(bias[:, 0:3 * P], 0.0).then_inc(s_vones, 1)
                    pool.wait_ge(s_vones, 2)
                    for i in range(2):
                        d = bias_of(i)[:, P * i:P * i + P]
                        g.affine_select(out=d, in_=d, compare_op=ALU.is_ge, fill=-BIG, base=0, pattern=[[-1, P]],
                                        channel_multiplier=1).then_inc(s_vones, 1)
                if (kind, n) == ("unit", UNIT[("cb", 1)]):
                    pool.wait_ge(s_need, 1)
                    g.partition_all_reduce(most, need, P, bass.bass_isa.ReduceOp.max).then_inc(s_most, 1)
                if (kind, n) == ("unit", UNIT[("av", 0)]):
                    pool.wait_ge(s_idx, NIH * len(IDX_BLOCKS))
                    g.memset(V[:, :, :, HD:2 * HD], 1.0).then_inc(s_vones, 1)
                if SPLITS.get((kind, n)) == "ak":
                    for t in range(NT):
                        section_low(g, pool, SPLITS[(kind, n)], t)
            for c in range(0, KT, 2):
                out_low(g, pool, c, s_woLp)

            def pair_square(t):
                pool.wait_ge(s_o, 4 * (t + 1))
                if t == 0:
                    g.memset(onesq[:], 1.0).then_inc(s_onesq, 1)
                else:
                    pool.wait_ge(s_yn, t)
                g.tensor_tensor(ysq[:], ya[:, t, :], ya[:, t, :], ALU.mult).then_inc(s_ysq, 1)

            def pair_scale(t):
                pool.wait_ge(s_yrs, 2 * t + 2)
                g.tensor_tensor(ya[:, t, :], ya[:, t, :], ysq[:], ALU.mult).then_inc(s_yn, 1)

            for t in range(NT):
                pair_square(t)
                pair_scale(t)
            for b in range(NB):
                pool.wait_ge(s_og, b + 1)
                pool.wait_ge(s_xe[b % 2], 16 * (b // 2 + 1))
                g.tensor_tensor(te[:, b % 2, :], te[:, b % 2, :], xe[:, b % 2, :], ALU.add).then_inc(s_res, 1)


INPUTS = ("x", "positions", "w_ada", "w_out", "norm_f", "b_gate", "w_ik", "w_units", "vecs", "ident_f", "ident_b",
          "pairs", "delta")


def kernel(x, c, positions, w_ada, b_ada, norm_in, w_in, conv_w, conv_b, gn_conv, gn_attn, w_out, norm_f):
    import ml_dtypes
    import concourse.bacc as bacc
    from concourse.bass_utils import run_bass_kernel_spmd

    def columns(v):
        return np.asarray(v).reshape(-1, P).T

    w_in = np.asarray(w_in)
    tiles = np.stack([w_in[:, STARTS[s] + P * t:STARTS[s] + P * t + P] for s, t in UNITS[1:]])
    freq = np.float32(500000.0) ** (-np.arange(ROPE // 2, dtype=np.float32) / np.float32(ROPE // 2))
    row = np.arange(P) % ROPE
    vecs = np.zeros((P, V_COLS), np.float32)
    for at, v in ((V_C, c), (V_NORM, norm_in), (V_BSH, b_ada[:D]), (V_BSC, b_ada[D:2 * D]), (V_CW, conv_w),
                  (V_CB, conv_b), (V_GC, gn_conv), (V_GA, gn_attn)):
        v = columns(v)
        vecs[:, at:at + v.shape[1]] = v
    vecs[:, V_FREQ] = freq[row % (ROPE // 2)]
    vecs[:, V_SIGN] = np.where(row < ROPE // 2, -1.0, 1.0)
    vecs[:, V_EPS] = EPS
    group = np.arange(P) // HD
    arrays = {
        "x": x, "positions": positions, "w_ada": w_ada, "w_out": w_out, "norm_f": norm_f, "b_gate": b_ada[2 * D:],
        "w_ik": w_in[:, 4608:4680].reshape(KT, P, 72).transpose(1, 0, 2),
        "w_units": tiles.reshape(NU - 1, KT, P, P).transpose(0, 2, 1, 3),
        "vecs": vecs, "ident_f": np.eye(P, dtype=np.float32), "ident_b": np.eye(P).astype(ml_dtypes.bfloat16),
        "pairs": (group[:, None] == group[None, :]).astype(np.float32),
        "delta": (np.arange(16)[:, None, None] % NB == np.arange(NB)[None, :, None]).repeat(P, 2).astype(ml_dtypes.bfloat16),
    }
    arrays = {"in_" + k: np.ascontiguousarray(arrays[k]) for k in INPUTS}
    nc = bacc.Bacc("TRN2", target_bir_lowering=False, num_devices=1)
    aps = {k: nc.dram_tensor("in_" + k, arrays["in_" + k].shape, mybir.dt.from_np(arrays["in_" + k].dtype),
                             kind="ExternalInput").ap() for k in INPUTS}
    aps["out"] = nc.dram_tensor("out", (1, S, D), F32, kind="ExternalOutput").ap()
    build(nc, aps)
    return run_bass_kernel_spmd(nc, [arrays], core_ids=[0]).results[0]["out"]
```

```python
from contextlib import ExitStack

import numpy as np

import concourse.bass as bass
from concourse import mybir

P = 128
D = 1024
S = 1024
KT = D // P
NB = S // P
HD = 64
NH = 8
NIH = 8
NT = 4
ROPE = 16
TOPK = 256
ROUND = 8
HALF = 512
EPS = 1e-6
IDX_SCALE = float(HD) ** -0.5 * float(NIH) ** -0.5
ATT_SCALE = float(HD) ** -0.5
TAKEN = -3.0e38
FUTURE = -3.3e38
BIG = 1.0e30
MAGIC = 1.5 * 2.0 ** 23
PI = 3.1415925

F32 = mybir.dt.float32
F32R = mybir.dt.float32r
BF16 = mybir.dt.bfloat16
I32 = mybir.dt.int32
ALU = mybir.AluOpType
ACT = mybir.ActivationFunctionType

V_C, V_NORM, V_BSH, V_BSC = 0, 8, 16, 24
V_CW, V_CB, V_GC, V_GA = 32, 44, 48, 52
V_FREQ, V_SIGN, V_EPS, V_COLS = 56, 57, 58, 64


def two_pi_parts():
    left, parts = 2 * np.pi, []
    for _ in range(3):
        m, e = np.frexp(left)
        parts.append(float(np.round(m * 256) / 256 * 2.0 ** e))
        left -= parts[-1]
    return parts + [float(left)]


UNITS = ([("ik", 0)] + [("aq", t) for t in range(NT)] + [("iq", t) for t in range(NT)]
         + [("ak", t) for t in range(NT)] + [("av", t) for t in range(NT)]
         + [(s, t) for t in range(NT) for s in ("cc", "cu", "cb", "cz")] + [("az", t) for t in range(NT)])
NU = len(UNITS)
UNIT = {u: n for n, u in enumerate(UNITS)}
STARTS = {s: 512 * i for i, s in enumerate(("cb", "cc", "cu", "cz", "aq", "ak", "av", "az", "iq"))}
NRAW = 2


def schedule():
    after = {
        ("aq", 0): [("iwt", 0)],
        ("ak", 2): [("idx", 2), ("idx", 3)],
        ("ak", 3): [("idx", 4), ("idx", 5), ("idx", 6), ("idx", 7)],
        ("av", 2): [("vt", 0)],
        ("av", 3): [("vt", 1)],
        ("cc", 0): [("vt", 2)],
        ("cu", 0): [("vt", 3)],
    }
    for t in range(NT):
        n = UNIT[("cz", t)] + 1
        after.setdefault(UNITS[n], []).append(("cn", t))
    out = []
    for n, u in enumerate(UNITS):
        out.append(("unit", n))
        out += after.get(u, [])
    return out


SCHEDULE = schedule()
EARLY = UNIT[("av", 0)]
SPLITS = {("unit", UNIT[("iq", 1)]): "aq", ("unit", UNIT[("ak", 1)]): "iq", ("unit", UNIT[("cc", 0)]): "ak"}
SCORES_IN = {UNIT[("ak", 3)]: (2, 8), UNIT[("av", 0)]: (4, 0), UNIT[("av", 1)]: (6, 0)}
HL_POOL = (2, 5)
IDX_BLOCKS = range(TOPK // P, NB)
NI = len(IDX_BLOCKS)
HALVINGS = 10
SUMS_AFTER = {2: 0, 4: 1, 6: 2, 7: 3}
NPROB = 3
Y_ORDER = [(0, 0), (1, 0), (0, 1), (1, 1)] + [(b, part) for b in range(2, NB) for part in range(2)]
Y_AT = {y: n for n, y in enumerate(Y_ORDER)}
PV_LAG = 2
OUT_TILES = {1: (3,), 2: (4,), 3: (5,), 4: (6,), 5: (7,), 6: (0, 1), 7: (2,)}


def build(nc, a):
    with ExitStack() as ctx:
        base = 16512
        used = [0]

        def at(name, shape, dt, kb):
            off = base + int(kb * 1024)
            assert off % 32 == 0
            return nc.alloc_sbuf_tensor_at(name, shape, dt, offset=off)

        def sem(name):
            return ctx.enter_context(nc.semaphore(name))

        arena = ctx.enter_context(nc.sbuf_tensor("arena", [P, 207 * 256], F32))

        hH = at("hH", [P, KT, S], F32R, 0)
        hL = at("hL", [P, KT, S], F32R, 32)
        wo = at("wo", [P, KT, D], F32, 32)
        raw = at("raw", [P, NRAW, KT, P], F32, 64)
        wH = at("wH", [P, 2, KT, P], F32R, 76)
        wL = at("wL", [P, 2, KT, P], F32R, 84)
        bias = at("bias", [P, 36 * P], BF16, 92)
        score = at("score", [P, 33 * P], F32, 93.5)
        identF = at("identF", [P, P], F32, 110)
        pairs = at("pairs", [P, P], F32, 110.5)
        identB = at("identB", [P, P], BF16, 111)
        onesB = at("onesB", [16, P], BF16, 111.25)
        vec = at("vec", [P, V_COLS], F32, 111.5)
        wabs = at("wabs", [P, NB, NIH], F32, 111.75)
        wsgn = at("wsgn", [P, NB, NIH], F32, 112)
        small = at("small", [P, 64], F32, 112.25)
        onesF = at("onesF", [P, 1], F32, 112.5)
        m8 = at("m8", [P, ROUND], F32, 112.5625)
        mx = at("mx", [P, NB], F32, 112.625)
        mparts = at("mparts", [P, 2 * NB], BF16, 112.6875)
        srch = at("srch", [P, 64], F32, 112.75)
        lo, step, hi, cand, count, good, need, most = (srch[:, NI * k:NI * k + NI] for k in range(8))
        ramp = srch[:, 48:48 + ROUND]
        limit = srch[:, 56:56 + ROUND]
        rounds = at("rounds", [P, NI], I32, 112.75)
        above = at("above", [P, S], BF16, 205)
        csilu = small[:, 0:8]
        sumsq = small[:, 8:16]
        rstd = small[:, 16:24]
        shift = small[:, 24:32]
        amp = small[:, 32:40]
        fin = small[:, 40:48]
        finr = small[:, 48:56]
        xin = at("xin", [P, NB, D], F32, 113)
        xT = at("xT", [P, KT, S], F32, 145)
        wa = [at(f"wa{i}", [P, 2 * D], F32, kb) for i, kb in enumerate((177, 185, 93, 101))]
        acc = at("acc", [P, 2 * D], F32, 193)
        iqs = at("iqs", [P, NIH, S], F32R, 113)
        iks1 = at("iks1", [P, S], F32R, 145)
        iks2 = at("iks2", [P, S], F32R, 149)
        Taqk = at("Taqk", [P, NT, S], F32, 153)
        Tiq = at("Tiq", [P, NT, S], F32, 93.5)
        T = {"iq": Tiq, "aq": Taqk, "ak": Taqk}
        cx = at("cx", [P, S], F32, 169)
        cs = at("cs", [P, S], F32, 173)
        tabC = at("tabC", [P, S], F32, 177)
        tabS = at("tabS", [P, S], F32, 181)
        Tik = at("Tik", [P, S], F32, 185)
        hlH = [at(f"hlH{i}", [P, S], F32R, kb) for i, kb in enumerate((189, 72))]
        hlL = [at(f"hlL{i}", [P, S], F32R, kb) for i, kb in enumerate((193, 185))]
        relu = at("relu", [P, 2, S], F32, 197)
        posi = at("posi", [P, S], I32, 169)
        ang = at("ang", [P, S], F32, 173)
        turns = at("turns", [P, S], F32, 189)
        V = at("V", [P, NB, NT, 3 * HD], F32, 113)
        vst = at("vst", [P, 2, S], F32, 137)
        convc = at("convc", [P, S], F32, 145)
        convu = at("convu", [P, S], F32, 149)
        convs = at("convs", [P, 2 + S], F32, 153)
        conv0 = at("conv0", [P, S], F32, 157.25)
        conv1 = at("conv1", [P, S], F32, 161.5)
        convb = at("convb", [P, S], F32, 165.5)
        azs = at("azs", [P, NT, S], F32, 170)
        yconv = at("yconv", [P, NT, S], F32, 189)
        qs = [at(f"qs{i}", [P, S], F32R, kb) for i, kb in enumerate((145, 157, 0))]
        ks1 = [at(f"ks1_{i}", [P, S], F32R, kb) for i, kb in enumerate((149, 161, 4))]
        ks2 = [at(f"ks2_{i}", [P, S], F32R, kb) for i, kb in enumerate((153, 165, 8))]
        prob = at("prob", [P, NPROB, HALF], F32, 137)
        mrow = [at(f"mrow{i}", [16, NB, P], BF16, kb) for i, kb in enumerate((186, 143))]
        delta = at("delta", [16, NB, P], BF16, 205)
        ya = at("ya", [P, NT, S], F32, 64)
        rden = at("rden", [P, HALF], F32, 102)
        ysq = at("ysq", [P, S], F32, 104)
        onesq = at("onesq", [P, P], F32, 108)
        gw = at("gw", [P, 2, D], F32, 80)
        gate = at("gate", [P, D], F32, 88)
        yH = [at(f"yH{i}", [P, KT, P], F32R, 145 + 8 * i) for i in range(2)]
        yL = [at(f"yL{i}", [P, KT, P], F32R, kb) for i, kb in enumerate((149, 80))]
        normf = at("normf", [P, D], F32, 161)
        bgate = at("bgate", [P, D], F32, 84)
        xe = at("xe", [P, 2, D], F32, 113)
        oe = at("oe", [P, 2, D], F32, 121)
        te = at("te", [P, 2, D], F32, 129)

        ps = ctx.enter_context(nc.psum_tensor("ps", [P, 8, HALF], F32))

        def two(b):
            return ps[:, b:b + 2, :].rearrange("p b n -> p (b n)")

        dx = nc.dram_tensor("rope_x", [3, NH, ROPE, S], F32).ap()
        dp = nc.dram_tensor("rope_partner", [3, NH, ROPE, S], F32).ap()
        dr = nc.dram_tensor("rope_rotated", [3, NH, ROPE, S], F32).ap()
        dqk = nc.dram_tensor("qk_halves", [2, 2, NT, P, S], F32).ap()

        s_const = sem("s_const"); s_pos = sem("s_pos")
        s_x = [sem(f"s_x{t}") for t in range(NB)]
        s_wa = [sem(f"s_wa{i}") for i in range(4)]
        s_ones = sem("s_ones"); s_csilu = sem("s_csilu"); s_sumsq = sem("s_sumsq")
        s_var = sem("s_var"); s_std = sem("s_std"); s_xn = sem("s_xn")
        s_xtp = sem("s_xtp"); s_xt = sem("s_xt")
        s_acc = sem("s_acc"); s_modp = sem("s_modp")
        s_h = sem("s_h"); s_hH = sem("s_hH"); s_hL = sem("s_hL"); s_hLp = sem("s_hLp")
        s_red = sem("s_red"); s_trig = sem("s_trig"); s_tab = sem("s_tab")
        s_raw = [sem(f"s_raw{i}") for i in range(NRAW)]
        s_wH = sem("s_wH"); s_wL = sem("s_wL")
        s_unit = sem("s_unit"); s_evac = sem("s_evac")
        s_iwt = sem("s_iwt"); s_iw = sem("s_iw")
        s_cx = sem("s_cx"); s_rot = sem("s_rot"); s_back = sem("s_back"); s_bounce = sem("s_bounce")
        s_kiH = sem("s_kiH"); s_kiL = sem("s_kiL"); s_kidup = sem("s_kidup")
        s_splH = sem("s_splH"); s_splL = sem("s_splL")
        s_spill = [sem("s_spill0"), sem("s_spill1")]
        s_idx = sem("s_idx"); s_relu = sem("s_relu"); s_score = sem("s_score")
        s_caus = sem("s_caus"); s_round = sem("s_round"); s_mask = sem("s_mask")
        s_range = sem("s_range"); s_halve = sem("s_halve"); s_count = sem("s_count"); s_need = sem("s_need")
        s_most = sem("s_most")
        s_vt = sem("s_vt"); s_v = sem("s_v"); s_vones = sem("s_vones")
        s_cvs = sem("s_cvs"); s_cvt = sem("s_cvt"); s_cvy = sem("s_cvy"); s_cvq = sem("s_cvq")
        s_cvp = sem("s_cvp"); s_cvd = sem("s_cvd"); s_cvr = sem("s_cvr"); s_cvn = sem("s_cvn")
        s_pad = sem("s_pad"); s_onesq = sem("s_onesq")
        s_wo = sem("s_wo"); s_woH = sem("s_woH"); s_woL = sem("s_woL")
        s_stack = [sem(f"s_stack{i}") for i in range(3)]
        s_delta = sem("s_delta")
        s_lg = sem("s_lg"); s_mx = sem("s_mx"); s_mp = sem("s_mp"); s_mt = sem("s_mt"); s_mrow = sem("s_mrow")
        s_st = sem("s_st"); s_exp = sem("s_exp"); s_pv = sem("s_pv"); s_o = sem("s_o")
        s_ysq = sem("s_ysq"); s_yss = sem("s_yss"); s_yln = sem("s_yln"); s_yrs = sem("s_yrs")
        s_yn = sem("s_yn"); s_ya = sem("s_ya")
        s_gw = [sem("s_gw0"), sem("s_gw1")]
        s_gacc = sem("s_gacc"); s_gp = sem("s_gp"); s_gate = sem("s_gate"); s_nf = sem("s_nf"); s_bg = sem("s_bg")
        s_yH = sem("s_yH"); s_yL = sem("s_yL"); s_op = sem("s_op"); s_og = sem("s_og")
        s_xe = [sem("s_xe0"), sem("s_xe1")]
        s_res = sem("s_res"); s_fsq = sem("s_fsq"); s_fv = sem("s_fv"); s_fs = sem("s_fs")
        s_fin = sem("s_fin")
        s_out = [sem("s_out0"), sem("s_out1")]
        own_act = sem("own_act"); own_dve = sem("own_dve"); own_pool = sem("own_pool")

        SECT = {"aq": 0, "iq": 1, "ak": 2}
        NBOUNCE = 6

        def score_of(i):
            o = (i * (i + 1) // 2 - 3) * P
            return score[:, o:o + (i + 1) * P]

        def bias_of(i):
            o = (i * (i + 1) // 2) * P
            return bias[:, o:o + (i + 1) * P]

        def rows(h):
            return slice(HD * (h % 2), HD * (h % 2) + HD)

        def chunks(sb):
            return [(j, max(0, j - 4 * sb)) for j in range(4 * sb + 4)]

        MAXIMA, SUMS = -1, -2
        ST = []
        for h in range(NH):
            if h == 0:
                ST.append((0, MAXIMA, 0, 0))
            for sb in range(2):
                ST += [(h, sb, j, c) for j, c in chunks(sb)]
            if h + 1 < NH:
                ST.insert(-1, (h + 1, MAXIMA, 0, 0))
            if h in SUMS_AFTER:
                ST += [(SUMS_AFTER[h], SUMS, half, 0) for half in range(2)]
        ST_AT = {u[:3]: n for n, u in enumerate(ST)}
        PV = [u for u in ST if u[1] >= 0]
        PV_AT = {u[:3]: n for n, u in enumerate(PV)}

        def section_low(engine, waits, sec, t):
            m = NT * SECT[sec] + t
            waits.wait_ge(s_splH, m + 1)
            engine.tensor_tensor(hlL[m % 2][:], T[sec][:, t, :], hlH[m % 2][:].bitcast(F32),
                                 ALU.subtract).then_inc(s_splL, 1)

        def low_h(engine, waits, kt, done):
            waits.wait_ge(s_h, kt + 1)
            waits.wait_ge(s_hH, kt + 1)
            engine.tensor_tensor(hL[:, kt, :], xT[:, kt, :], hH[:, kt, :].bitcast(F32), ALU.subtract).then_inc(done, 1)

        block = ctx.enter_context(nc.Block())

        @block.sync
        def _(sp):
            sp.dma_start(vec[:], a["vecs"]).then_inc(s_const, 16)
            sp.dma_start(identF[:], a["ident_f"]).then_inc(s_const, 16)
            sp.dma_start(pairs[:], a["pairs"]).then_inc(s_const, 16)
            sp.dma_start(identB[:], a["ident_b"]).then_inc(s_const, 16)

            def load(n):
                if NRAW <= n < NU + NRAW:
                    sp.wait_ge(s_wL, n - NRAW + 1)
                if n == 0:
                    sp.dma_start(raw[:, 0, :, 0:72], a["w_ik"]).then_inc(s_raw[0], 16)
                else:
                    sp.dma_start(raw[:, n % NRAW, :, :], a["w_units"][n - 1]).then_inc(s_raw[n % NRAW], 16)

            w_ada = a["w_ada"].rearrange("(k p) n -> k p n", p=P)
            for kt in range(KT):
                if kt == 3:
                    for t in range(NB):
                        sp.dma_start(xin[:, t, :], a["x"][0, P * t:P * t + P, :]).then_inc(s_x[t], 16)
                if kt >= 4:
                    sp.wait_ge(s_acc, kt - 3)
                sp.dma_start(wa[kt % 4][:], w_ada[kt, :, 0:2 * D]).then_inc(s_wa[kt % 4], 16)
                if kt in (3, 4):
                    load(kt - 3)

            load(NRAW)
            sp.wait_ge(s_hL, KT - len(HL_POOL))
            sp.wait_ge(s_hLp, len(HL_POOL))
            sp.dma_start(posi[:], a["positions"][0:1, :].broadcast_to([P, S])).then_inc(s_pos, 16)

            def rope_out(sec):
                sp.wait_ge(s_evac, UNIT[(sec, NT - 1)] + 1)
                k = SECT[sec]
                for odd in range(2):
                    b = HD * odd
                    for (lo, n, dst, to) in ((0, 16, dx, 0), (0, 8, dp, 8), (8, 8, dp, 0)):
                        sp.dma_start(dst[k, odd::2, to:to + n, :].rearrange("t r s -> r t s"),
                                     T[sec][b + lo:b + lo + n, :, :]).then_inc(s_bounce, 16)
                sp.wait_ge(s_bounce, 16 * NBOUNCE * (k + 1) + 32 * k)
                sp.wait_ge(s_back, 16 if k == 0 else 16 + 32 * k)
                sp.dma_start(cx[:], dx[k].rearrange("h r s -> (h r) s")).then_inc(s_cx, 16)
                sp.dma_start(cs[:], dp[k].rearrange("h r s -> (h r) s")).then_inc(s_cx, 16)

            def rope_back(sec):
                k = SECT[sec]
                sp.wait_ge(s_rot, k + 2)
                sp.dma_start(dr[k].rearrange("h r s -> (h r) s"), cx[:]).then_inc(s_bounce, 32)
                sp.wait_ge(s_bounce, (16 * NBOUNCE + 32) * (k + 1))
                for odd in range(2):
                    sp.dma_start(T[sec][HD * odd:HD * odd + ROPE, :, :],
                                 dr[k, odd::2, :, :].rearrange("t r s -> r t s")).then_inc(s_back, 16)

            def spill(sec):
                for t in range(NT):
                    m = NT * SECT[sec] + t
                    sp.wait_ge(s_splH, m + 1)
                    sp.wait_ge(s_splL, m + 1)
                    for half, src in enumerate((hlH[m % 2], hlL[m % 2])):
                        if sec == "iq":
                            for odd in range(2):
                                sp.dma_start(iqs[HD * half:HD * half + HD, 2 * t + odd, :].bitcast(F32),
                                             src[HD * odd:HD * odd + HD, :].bitcast(F32)).then_inc(s_spill[m % 2], 16)
                        else:
                            sp.dma_start(dqk[("aq", "ak").index(sec), half, t], src[:].bitcast(F32)).then_inc(s_spill[m % 2], 32)

            for kind, n in SCHEDULE:
                if kind != "unit":
                    continue
                if 1 <= n < NU - NRAW:
                    load(n + NRAW)
                if UNITS[n] == ("aq", 0):
                    sp.wait_ge(s_evac, 1)
                    sp.wait_ge(s_tab, 1)
                    sp.dma_start(cx[0:16, :], Tik[0:16, :]).then_inc(s_cx, 16)
                    sp.dma_start(cs[0:8, :], Tik[8:16, :]).then_inc(s_cx, 16)
                    sp.dma_start(cs[8:16, :], Tik[0:8, :]).then_inc(s_cx, 16)
                    sp.wait_ge(s_rot, 1)
                    sp.dma_start(Tik[0:16, :], cx[0:16, :]).then_inc(s_back, 16)
                if UNITS[n] == ("aq", 2):
                    sp.wait_ge(s_kiH, 1)
                    sp.dma_start(iks1[HD:P, :].bitcast(F32), iks1[0:HD, :].bitcast(F32)).then_inc(s_kidup, 16)
                    sp.wait_ge(s_kiL, 1)
                    sp.dma_start(iks2[HD:P, :].bitcast(F32), iks2[0:HD, :].bitcast(F32)).then_inc(s_kidup, 16)
                sec, t = UNITS[n]
                if sec in SECT and t == NT - 1:
                    rope_out(sec)
                if UNITS[n] in (("iq", 0), ("ak", 0), ("av", 2)):
                    rope_back({"iq": "aq", "ak": "iq", "av": "ak"}[sec])
                if UNITS[n] in (("iq", 2), ("ak", 2), ("cu", 0)):
                    spill({"iq": "aq", "ak": "iq", "cu": "ak"}[sec])

            sp.wait_ge(s_cvn, NT)
            sp.wait_ge(s_mask, NI)
            sp.dma_start(delta[:], a["delta"]).then_inc(s_delta, 16)
            for i in range(2):
                sp.wait_ge(s_spill[i], 16 * (4 * 2 + 4 * 4))
            for h in range(NH):
                if h == 2:
                    sp.wait_ge(s_unit, NU)
                if h >= 3:
                    sp.wait_ge(s_st, PV_AT[(h - 3, 1, NB - 1)] + 1)
                t, r = h // 2, rows(h)
                for i, dst in enumerate((qs, ks1, ks2)):
                    for half in range(2):
                        part = half if i == 0 else i - 1
                        sp.dma_start(dst[h % 3][HD * half:HD * half + HD, :].bitcast(F32),
                                     dqk[min(i, 1), part, t, r, :]).then_inc(s_stack[h % 3], 16)
                if h == 2:
                    for ct in range(KT):
                        sp.dma_start(wo[:, ct, :], a["w_out"][P * ct:P * ct + P, :]).then_inc(s_wo, 16)
                if h >= 4:
                    for kt in (2 * h - 8, 2 * h - 7):
                        if kt >= 2:
                            sp.wait_ge(s_gacc, kt - 1)
                        sp.dma_start(gw[:, kt % 2, :], w_ada[kt, :, 2 * D:3 * D]).then_inc(s_gw[kt % 2], 16)

            sp.wait_ge(s_gacc, KT)
            sp.dma_start(bgate[:], a["b_gate"].rearrange("(o n) -> o n", o=1).broadcast_to([P, D])).then_inc(s_bg, 16)
            sp.wait_ge(s_pv, len(PV))
            sp.dma_start(normf[:], a["norm_f"].rearrange("(o n) -> o n", o=1).broadcast_to([P, D])).then_inc(s_nf, 16)
            for b in range(2):
                sp.dma_start(xe[:, b, :], a["x"][0, P * b:P * b + P, :]).then_inc(s_xe[b], 16)
            for b in range(NB):
                sp.wait_ge(s_fin, b + 1)
                sp.dma_start(a["out"][0, P * b:P * b + P, :], oe[:, b % 2, :]).then_inc(s_out[b % 2], 16)
                if b + 2 < NB:
                    sp.wait_ge(s_res, b + 1)
                    sp.dma_start(xe[:, b % 2, :], a["x"][0, P * (b + 2):P * (b + 3), :]).then_inc(s_xe[b % 2], 16)
            for i in range(2):
                sp.wait_ge(s_out[i], 16 * (NB // 2))

        @block.tensor
        def _(pe):
            pe.wait_ge(s_const, 16 * 4)
            for kt in range(KT):
                if kt == 0:
                    pe.wait_ge(s_xn, NB)
                if kt >= 4:
                    pe.wait_ge(s_xt, kt - 3)
                for t in range(NB):
                    mm = pe.transpose(two(2 * (kt % 4))[:, P * t:P * t + P], xin[:, t, P * kt:P * kt + P], identF[:])
                mm.then_inc(s_xtp, 1)
            pe.wait_ge(s_acc, KT)
            pe.wait_ge(s_ones, 1)
            pe.wait_ge(s_xt, KT)
            for j in range(2 * KT):
                mm = pe.matmul(ps[:, 0, j:j + 1], acc[:, P * j:P * j + P], onesF[:], start=(j == 0), stop=True,
                               skip_group_check=True)
            mm.then_inc(s_modp, 1)

            def unit(n):
                m = 72 if n == 0 else P
                pe.wait_ge(s_wH, n + 1)
                pe.wait_ge(s_wL, n + 1)
                if n >= 2:
                    pe.wait_ge(s_evac, n - 1)
                if n == 0:
                    pe.wait_ge(s_h, 1)
                b, first = SCORES_IN.get(n, (0, 0))
                scored = 0
                for half in range(2):
                    out = ps[0:m, 2 * (n % 2) + half, :]
                    cols = slice(HALF * half, HALF * half + HALF)
                    for kt in range(KT):
                        if n == 0 and half == 0:
                            pe.wait_ge(s_hH, kt + 1)
                            if kt in HL_POOL:
                                pe.wait_ge(s_hLp, HL_POOL.index(kt) + 1)
                            else:
                                pe.wait_ge(s_hL, kt + 1 - sum(k < kt for k in HL_POOL))
                        pe.matmul(out, wH[:, n % 2, kt, 0:m], hH[:, kt, cols], start=(kt == 0), stop=False)
                        pe.matmul(out, wH[:, n % 2, kt, 0:m], hL[:, kt, cols], start=False, stop=False)
                        mm = pe.matmul(out, wL[:, n % 2, kt, 0:m], hH[:, kt, cols], start=False, stop=(kt == KT - 1))
                        at_step = KT * half + kt + 1
                        while b and at_step > first and scored * (2 * KT - first) < 2 * NIH * (at_step - first):
                            index_scores(b + scored // NIH, scored % NIH)
                            scored += 1
                mm.then_inc(s_unit, 1)

            def index_scores(i, h):
                n = (i + 1) * P
                u = NIH * (i - 2) + h
                if u == 0:
                    pe.wait_ge(s_kidup, 32)
                    pe.wait_ge(s_spill[0], 64 * 4)
                    pe.wait_ge(s_spill[1], 64 * 4)
                    pe.wait_ge(s_iw, 1)
                if u >= 2:
                    pe.wait_ge(s_relu, u - 1)
                dst = two(4 + 2 * (u % 2))
                for o in range(0, n, HALF):
                    e = min(n, o + HALF)
                    pe.matmul(dst[:, o:e], iqs[:, h, P * i:P * i + P], iks1[:, o:e], start=True, stop=False)
                    mm = pe.matmul(dst[:, o:e], iqs[:, h, P * i:P * i + P], iks2[:, o:e], start=False, stop=True)
                mm.then_inc(s_idx, 1)

            for kind, n in SCHEDULE:
                if kind == "unit":
                    unit(n)
                elif kind == "iwt":
                    pe.wait_ge(s_evac, 1)
                    for b in range(NB):
                        mm = pe.transpose(ps[:, 4, NIH * b:NIH * b + NIH], Tik[64:72, P * b:P * b + P], identF[64:72, 64:72])
                    mm.then_inc(s_iwt, 1)
                elif kind == "vt":
                    pe.wait_ge(s_evac, UNIT[("av", n)] + 1)
                    if n == 0:
                        pe.wait_ge(s_relu, 8 * len(IDX_BLOCKS))
                    if n >= 2:
                        pe.wait_ge(s_v, n - 1)
                    for b in range(NB):
                        mm = pe.transpose(two(4 + 2 * (n % 2))[:, P * b:P * b + P], vst[:, n % 2, P * b:P * b + P], identF[:])
                    mm.then_inc(s_vt, 1)
                elif kind == "cn":
                    pe.wait_ge(s_cvq, n + 1)
                    if n == 0:
                        pe.wait_ge(s_v, NT)
                    else:
                        pe.wait_ge(s_cvd, n)
                    for half in range(2):
                        mm = pe.matmul(ps[:, 4 + half, :], pairs[:], conv0[:, HALF * half:HALF * half + HALF], start=True, stop=True)
                    mm.then_inc(s_cvp, 1)

            def logits(h, x):
                if x == 0:
                    pe.wait_ge(s_stack[h % 3], 96 * (h // 3 + 1))
                i = NB - 1 - x
                u = NB * h + x
                n = (i + 1) * P
                if u == 0:
                    pe.wait_ge(s_evac, NU)
                if u >= 2:
                    pe.wait_ge(s_mx, u - 1)
                dst = two(2 * (u % 2))
                q = qs[h % 3][:, P * i:P * i + P]
                for o in range(0, n, HALF):
                    e = min(n, o + HALF)
                    pe.matmul(dst[:, o:e], q, ks1[h % 3][:, o:e], start=True, stop=False)
                    mm = pe.matmul(dst[:, o:e], q, ks2[h % 3][:, o:e], start=False, stop=True)
                mm.then_inc(s_lg, 1)

            def st_slot(u):
                if u == 0:
                    pe.wait_ge(s_cvd, NT)
                if u >= 2:
                    hh, sb, j, _ = ST[u - 2]
                    if sb == MAXIMA:
                        pe.wait_ge(s_mrow, hh + 1)
                    elif sb == SUMS:
                        pe.wait_ge(s_yln, 2 * hh + j + 1)
                    else:
                        pe.wait_ge(s_exp, PV_AT[(hh, sb, j)] + 1)
                return 4 + u % 2

            def maxima(h):
                bank = st_slot(ST_AT[(h, -1, 0)])
                pe.wait_ge(s_mp, h + 1)
                pe.transpose(ps[0:16, bank, :].bitcast(BF16)[:, 0:P], mparts[:], identB[:]).then_inc(s_mt, 1)

            def scores_t(u):
                h, sb, j, c = ST[u]
                if (sb, j) == (0, 0):
                    pe.wait_ge(s_mrow, h + 1)
                bank = st_slot(u)
                out = ps[:, bank, P * c:HALF]
                cols = slice(HALF * sb + P * c, HALF * sb + HALF)
                keys = slice(P * j, P * j + P)
                pe.matmul(out, ks1[h % 3][:, keys], qs[h % 3][:, cols], start=True, stop=False, skip_group_check=True)
                pe.matmul(out, ks2[h % 3][:, keys], qs[h % 3][:, cols], start=False, stop=False, skip_group_check=True)
                for b in range(c, 4):
                    i = 4 * sb + b
                    if i >= 2 or i == j:
                        pe.matmul(ps[:, bank, P * b:P * b + P], bias_of(i)[:, keys], identB[:], start=False, stop=False,
                                  skip_group_check=True)
                pe.matmul(out, onesB[:], mrow[h % 2][:, 4 * sb + c:4 * sb + 4, :].rearrange("p b n -> p (b n)"), start=False,
                          stop=True, skip_group_check=True).then_inc(s_st, 1)

            def values(k):
                h, sb, j, c = PV[k]
                pe.wait_ge(s_exp, k + 1)
                if j == 0 and 2 * h + sb >= 2:
                    pe.wait_ge(s_o, 2 * h + sb - 1)
                w = V[:, j, h // 2, HD * (h % 2):HD * (h % 2) + P]
                pe.matmul(ps[:, 6 + sb, P * c:HALF], w, prob[:, k % NPROB, P * c:HALF], start=(j == 0),
                          stop=(j == 4 * sb + 3), skip_group_check=True).then_inc(s_pv, 1)

            def group_sums(t):
                pe.wait_ge(s_ysq, t + 1)
                for half in range(2):
                    bank = st_slot(ST_AT[(t, SUMS, half)])
                    pe.matmul(ps[:, bank, :], pairs[:], ysq[:, HALF * half:HALF * half + HALF], start=True,
                              stop=True).then_inc(s_yss, 1)

            def gate_rows():
                pe.wait_ge(s_gacc, KT)
                pe.wait_ge(s_onesq, 1)
                pe.wait_ge(s_mx, NB * NH)
                for half in range(2):
                    mm = pe.matmul(ps[:, 2 + half, :], onesq[:], gate[:, HALF * half:HALF * half + HALF], start=True, stop=True)
                mm.then_inc(s_gp, 1)

            pe.wait_ge(s_vones, 5)
            pe.wait_ge(s_mask, len(IDX_BLOCKS))
            for x in range(NB):
                logits(0, x)
            maxima(0)
            count = len(chunks(0)) + len(chunks(1))
            for h in range(NH):
                for x in range(count):
                    k = count * h + x
                    if x == count - 1 and h + 1 < NH:
                        maxima(h + 1)
                    scores_t(ST_AT[PV[k][:3]])
                    if k >= PV_LAG:
                        values(k - PV_LAG)
                    if x < NB and h + 1 < NH:
                        logits(h + 1, x)
                    if (h, x) == (NH - 1, 1):
                        gate_rows()
                if h in SUMS_AFTER and h < NH - 1:
                    group_sums(SUMS_AFTER[h])
            for k in range(count * NH - PV_LAG, count * NH):
                values(k)
            pe.wait_ge(s_woL, KT)
            pe.wait_ge(s_woH, KT)

            def out_part(b, part):
                n = Y_AT[(b, part)]
                pe.wait_ge(s_yH, n + 1)
                pe.wait_ge(s_yL, n + 1)
                for half in range(2):
                    out = ps[:, 2 * (b % 2) + half, :]
                    cols = slice(HALF * half, HALF * half + HALF)
                    for ct in range(NT * part, NT * part + NT):
                        pe.matmul(out, yH[b % 2][:, ct, :], hH[:, ct, cols], start=(ct == 0), stop=False)
                        pe.matmul(out, yH[b % 2][:, ct, :], hL[:, ct, cols], start=False, stop=False)
                        mm = pe.matmul(out, yL[b % 2][:, ct, :], hH[:, ct, cols], start=False, stop=(ct == KT - 1))
                if part:
                    mm.then_inc(s_op, 1)

            out_part(0, 0)
            group_sums(NT - 1)
            pe.wait_ge(s_gate, 1)
            out_part(1, 0)
            out_part(0, 1)
            out_part(1, 1)
            for b in range(2, NB):
                pe.wait_ge(s_og, b - 1)
                out_part(b, 0)
                out_part(b, 1)

        @block.scalar
        def _(act):
            A = nc.scalar.activation
            act.wait_ge(s_const, 16 * 4)
            A(csilu, vec[:, V_C:V_C + KT], ACT.Silu).then_inc(s_csilu, 1)
            for t in range(NB):
                act.wait_ge(s_x[t], 16)
                if t >= 4:
                    act.wait_ge(s_sumsq, t - 3)
                A(two(2 * (t % 4)), xin[:, t, :], ACT.Square, accum_out=sumsq[:, t:t + 1]).then_inc(s_sumsq, 1)
            act.wait_ge(s_var, 1)
            A(rstd, sumsq, ACT.Sqrt).then_inc(s_std, 1)
            for kt in range(KT):
                act.wait_ge(s_xtp, kt + 1)
                A(xT[:, kt, :], two(2 * (kt % 4)), ACT.Copy).then_inc(s_xt, 1)

            def split_high(n):
                act.wait_ge(s_raw[n % NRAW], 16 * (n // NRAW + 1))
                if n >= 2:
                    act.wait_ge(s_unit, n - 1)
                m = 72 if n == 0 else P
                A(wH[:, n % 2, :, 0:m], raw[:, n % NRAW, :, 0:m], ACT.Copy).then_inc(s_wH, 1)

            split_high(0)
            split_high(1)
            for kt in range(KT):
                act.wait_ge(s_h, kt + 1)
                A(hH[:, kt, :], xT[:, kt, :], ACT.Copy).then_inc(s_hH, 1)

            def evacuate(n):
                sec, t = UNITS[n]
                act.wait_ge(s_unit, n + 1)
                src = two(2 * (n % 2))
                if sec == "ik":
                    A(Tik[0:72, :], src[0:72, :], ACT.Copy).then_inc(s_evac, 1)
                elif sec in SECT:
                    if sec == "ak" and t == 0:
                        act.wait_ge(s_splL, NT)
                    A(T[sec][:, t, :], src, ACT.Copy).then_inc(s_evac, 1)
                elif sec == "av":
                    if t == 0:
                        act.wait_ge(s_idx, NIH * len(IDX_BLOCKS))
                    if t >= 2:
                        act.wait_ge(s_vt, t - 1)
                    A(vst[:, t % 2, :], src, ACT.Copy).then_inc(s_evac, 1)
                elif sec == "cc":
                    if t >= 1:
                        act.wait_ge(s_cvs, t)
                    A(convc[:], src, ACT.Copy).then_inc(s_evac, 1)
                elif sec == "cu":
                    A(convu[:], src, ACT.Copy).then_inc(s_evac, 1)
                elif sec == "cb":
                    if t == 0:
                        act.wait_ge(s_splL, 3 * NT)
                    else:
                        act.wait_ge(s_cvn, t)
                    A(convb[:], src, ACT.Copy).then_inc(s_evac, 1)
                elif sec == "cz":
                    if t == 0:
                        act.wait_ge(s_spill[0], 16 * 24)
                        act.wait_ge(s_spill[1], 16 * 24)
                    A(yconv[:, t, :], src, ACT.Silu).then_inc(s_evac, 1)
                elif sec == "az":
                    A(azs[:, t, :], src, ACT.Silu).then_inc(s_evac, 1)

            def taps(t):
                act.wait_ge(s_cvs, t + 1)
                A(conv0[:], convs[:, 2:2 + S], ACT.Identity, bias=vec[:, V_CB + t:V_CB + t + 1],
                  scale=vec[:, V_CW + 8 + t:V_CW + 9 + t]).then_inc(s_cvt, 1)
                A(conv1[:], convs[:, 1:1 + S], ACT.Copy, scale=vec[:, V_CW + 4 + t:V_CW + 5 + t]).then_inc(s_cvt, 1)
                act.wait_ge(s_cvy, 2 * t + 1)
                A(conv1[:], convs[:, 0:S], ACT.Copy, scale=vec[:, V_CW + t:V_CW + 1 + t]).then_inc(s_cvt, 1)

            evacuate(0)
            split_high(2)
            act.wait_ge(s_red, 1)
            A(tabS[:], ang[:], ACT.Sin).then_inc(s_trig, 1)
            A(turns[:], ang[:], ACT.Abs).then_inc(own_act, 1)
            act.wait_ge(s_red, 2)
            A(tabC[:], turns[:], ACT.Sin).then_inc(s_trig, 1)
            for kind, n in SCHEDULE[1:]:
                if kind == "unit":
                    evacuate(n)
                    if n + 2 < NU and n != EARLY:
                        split_high(n + 2)
                    sec, t = UNITS[n]
                    if sec == "cb":
                        taps(t)
                    if sec == "cz":
                        act.wait_ge(s_cvy, 2 * t + 2)
                        A(conv0[:], convb[:], ACT.Square).then_inc(s_cvq, 1)
                    if UNITS[n] == ("aq", 1):
                        act.wait_ge(s_back, 16)
                        A(iks1[0:HD, :], Tik[0:HD, :], ACT.Copy).then_inc(s_kiH, 1)
                elif kind == "idx":
                    for h in range(NIH):
                        u = NIH * (n - 2) + h
                        act.wait_ge(s_idx, u + 1)
                        if u >= 2:
                            act.wait_ge(s_score, u - 1)
                        w = (n + 1) * P
                        A(relu[:, u % 2, 0:w], two(4 + 2 * (u % 2))[:, 0:w], ACT.Relu, scale=wabs[:, n, h:h + 1]).then_inc(s_relu, 1)
                    if n == 5:
                        split_high(EARLY + 2)
                elif kind == "vt":
                    act.wait_ge(s_vt, n + 1)
                    src = two(4 + 2 * (n % 2)).rearrange("p (b g d) -> p b g d", b=NB, g=2)
                    for g in range(2):
                        mm = A(V[:, :, n, 2 * HD * g:2 * HD * g + HD], src[:, :, g, :], ACT.Copy)
                    mm.then_inc(s_v, 1)
                elif kind == "cn":
                    act.wait_ge(s_cvp, n + 1)
                    A(conv1[:], two(4), ACT.Ln, scale=1.0 / HD, bias=vec[:, V_EPS:V_EPS + 1]).then_inc(s_cvd, 1)
                    act.wait_ge(s_cvd, n + 1)
                    A(conv1[:], conv1[:], ACT.Exp, scale=-0.5).then_inc(s_cvr, 1)
                if (kind, n) in SPLITS:
                    sec = SPLITS[(kind, n)]
                    for t in range(NT):
                        m = NT * SECT[sec] + t
                        if t == 0:
                            act.wait_ge(s_back, 16 + 32 * (SECT[sec] + 1))
                        if m >= 2:
                            act.wait_ge(s_spill[m % 2], 64 * (m // 2))
                        A(hlH[m % 2][:], T[sec][:, t, :], ACT.Copy).then_inc(s_splH, 1)

            def exps(h):
                for sb in range(2):
                    for j, c in chunks(sb):
                        if sb == 0 and j in (1, 3) and j // 2 < len(OUT_TILES.get(h, ())):
                            act.wait_ge(s_wo, 16 * KT)
                            ct = OUT_TILES[h][j // 2]
                            A(hH[:, ct, :], wo[:, ct, :], ACT.Copy).then_inc(s_woH, 1)
                        k = PV_AT[(h, sb, j)]
                        act.wait_ge(s_st, k + 1)
                        if k == 0:
                            act.wait_ge(s_vt, NT)
                        if k >= NPROB:
                            act.wait_ge(s_pv, k - NPROB + 1)
                        A(prob[:, k % NPROB, P * c:HALF], ps[:, 4 + ST_AT[(h, sb, j)] % 2, P * c:HALF], ACT.Exp,
                          scale=ATT_SCALE).then_inc(s_exp, 1)

            def pair_rstd(t):
                for half in range(2):
                    act.wait_ge(s_yss, 2 * t + half + 1)
                    z = ysq[:, HALF * half:HALF * half + HALF]
                    A(z, ps[:, 4 + ST_AT[(t, SUMS, half)] % 2, :], ACT.Ln, scale=1.0 / HD,
                      bias=vec[:, V_EPS:V_EPS + 1]).then_inc(s_yln, 1)
                for half in range(2):
                    z = ysq[:, HALF * half:HALF * half + HALF]
                    act.wait_ge(s_yln, 2 * t + half + 1)
                    A(z, z, ACT.Exp, scale=-0.5).then_inc(s_yrs, 1)

            def high(b, part):
                if b >= 2:
                    act.wait_ge(s_op, b - 1)
                if part:
                    act.wait_ge(s_ya, NT)
                A(yH[b % 2][:, NT * part:NT * part + NT, :], (yconv, ya)[part][:, :, P * b:P * b + P], ACT.Copy).then_inc(s_yH, 1)

            for h in range(NH):
                exps(h)
                if h == NH - 2:
                    act.wait_ge(s_gacc, KT)
                    high(0, 0)
                    high(1, 0)
                if h in SUMS_AFTER:
                    pair_rstd(SUMS_AFTER[h])
            high(0, 1)
            high(1, 1)
            for b in range(NB):
                if b + 2 < NB:
                    high(b + 2, 0)
                    high(b + 2, 1)
                act.wait_ge(s_res, b + 1)
                if b >= 2:
                    act.wait_ge(s_out[b % 2], 16 * (b // 2))
                A(oe[:, b % 2, :], te[:, b % 2, :], ACT.Square, accum_out=fin[:, b:b + 1]).then_inc(s_fsq, 1)
                act.wait_ge(s_fv, b + 1)
                A(finr[:, b:b + 1], fin[:, b:b + 1], ACT.Sqrt).then_inc(s_fs, 1)

        @block.vector
        def _(dve):
            v = nc.vector
            chain = [0]

            def link(ins):
                chain[0] += 1
                ins.then_inc(own_dve, 1)
                dve.wait_ge(own_dve, chain[0])

            v.memset(onesF[:], 1.0).then_inc(s_ones, 1)
            for r in range(ROUND):
                v.memset(ramp[:, r:r + 1], float(r)).then_inc(s_ones, 1)
            dve.wait_ge(s_csilu, 1)

            def ada_sum(kt):
                dve.wait_ge(s_wa[kt % 4], 16 * (kt // 4 + 1))
                if kt == 0:
                    v.tensor_scalar(acc[:], wa[0][:], csilu[:, 0:1], None, ALU.mult).then_inc(s_acc, 1)
                else:
                    dve.wait_ge(s_acc, kt)
                    v.scalar_tensor_tensor(acc[:], wa[kt % 4][:], csilu[:, kt:kt + 1], acc[:], ALU.mult, ALU.add).then_inc(s_acc, 1)

            for kt in range(3):
                ada_sum(kt)
            dve.wait_ge(s_sumsq, NB)
            v.tensor_scalar(sumsq, sumsq, 1.0 / D, EPS, ALU.mult, ALU.add).then_inc(s_var, 1)
            dve.wait_ge(s_std, 1)
            link(v.reciprocal(rstd, rstd))
            for t in range(NB):
                v.tensor_scalar(xin[:, t, :], xin[:, t, :], rstd[:, t:t + 1], None, ALU.mult).then_inc(s_xn, 1)
            for kt in range(3, KT):
                ada_sum(kt)
            dve.wait_ge(s_modp, 1)
            v.tensor_tensor(shift, ps[:, 0, 0:KT], vec[:, V_BSH:V_BSH + KT], ALU.add)
            link(v.tensor_tensor(amp, ps[:, 0, KT:2 * KT], vec[:, V_BSC:V_BSC + KT], ALU.add))
            link(v.scalar_tensor_tensor(amp, amp, 1.0, vec[:, V_NORM:V_NORM + KT], ALU.add, ALU.mult))
            for kt in range(KT + 1):
                if kt < KT:
                    dve.wait_ge(s_xt, kt + 1)
                    v.tensor_scalar(xT[:, kt, :], xT[:, kt, :], amp[:, kt:kt + 1], shift[:, kt:kt + 1], ALU.mult, ALU.add).then_inc(s_h, 1)
                if kt >= 1 and kt - 1 not in HL_POOL:
                    low_h(v, dve, kt - 1, s_hL)

            dve.wait_ge(s_pos, 16)
            link(v.tensor_copy(ang[:], posi[:]))
            link(v.tensor_scalar(ang[:], ang[:], vec[:, V_FREQ:V_FREQ + 1], None, ALU.mult))
            link(v.tensor_scalar(turns[:], ang[:], 1.0 / (2 * np.pi), MAGIC, ALU.mult, ALU.add))
            link(v.tensor_scalar(turns[:], turns[:], MAGIC, None, ALU.subtract))
            for part in two_pi_parts():
                link(v.scalar_tensor_tensor(ang[:], turns[:], -part, ang[:], ALU.mult, ALU.add))
            v.tensor_scalar(ang[:], ang[:], PI, -PI, ALU.min, ALU.max).then_inc(s_red, 1)
            dve.wait_ge(own_act, 1)
            v.tensor_scalar(turns[:], turns[:], -1.0, float(np.pi / 2), ALU.mult, ALU.add).then_inc(s_red, 1)
            dve.wait_ge(s_trig, 2)
            v.tensor_scalar(tabS[:], tabS[:], vec[:, V_SIGN:V_SIGN + 1], None, ALU.mult).then_inc(s_tab, 1)
            dve.wait_ge(s_tab, 1)

            def rotate(k, n, count):
                dve.wait_ge(s_cx, count)
                v.tensor_tensor(cx[0:n, :], cx[0:n, :], tabC[0:n, :], ALU.mult)
                link(v.tensor_tensor(cs[0:n, :], cs[0:n, :], tabS[0:n, :], ALU.mult))
                v.tensor_tensor(cx[0:n, :], cx[0:n, :], cs[0:n, :], ALU.add).then_inc(s_rot, 1)

            rotate(0, ROPE, 48)
            dve.wait_ge(s_iwt, 1)
            iwp = ps[:, 4, 0:NB * NIH]
            wf = wabs[:].rearrange("p b h -> p (b h)")
            wg = wsgn[:].rearrange("p b h -> p (b h)")
            link(v.tensor_scalar(wg, iwp, 0.0, 2.0, ALU.is_ge, ALU.mult))
            link(v.tensor_scalar(wg, wg, 1.0, None, ALU.subtract))
            v.scalar_tensor_tensor(wf, iwp, IDX_SCALE, wg, ALU.mult, ALU.mult).then_inc(s_iw, 1)
            dve.wait_ge(s_kiH, 1)
            v.tensor_tensor(iks2[0:HD, :], Tik[0:HD, :], iks1[0:HD, :].bitcast(F32), ALU.subtract).then_inc(s_kiL, 1)
            rotate(1, P, 48 + 32)
            dve.wait_ge(s_kiL, 1)
            for t in range(NT):
                section_low(v, dve, "aq", t)
            rotate(2, P, 48 + 64)
            for t in range(NT):
                section_low(v, dve, "iq", t)
            dve.wait_ge(s_iw, 1)
            dve.wait_ge(s_splL, 2 * NT)
            for i in IDX_BLOCKS:
                n = (i + 1) * P
                for h in range(NIH):
                    u = NIH * (i - 2) + h
                    dve.wait_ge(s_relu, u + 1)
                    if h == 0:
                        v.tensor_scalar(score_of(i), relu[:, u % 2, 0:n], wsgn[:, i, 0:1], None, ALU.mult).then_inc(s_score, 1)
                    else:
                        dve.wait_ge(s_score, u)
                        v.scalar_tensor_tensor(score_of(i), relu[:, u % 2, 0:n], wsgn[:, i, h:h + 1], score_of(i),
                                               ALU.mult, ALU.add).then_inc(s_score, 1)
                b = i - IDX_BLOCKS[0]
                dve.wait_ge(s_score, NIH * (b + 1))
                v.tensor_reduce(lo[:, b:b + 1], score_of(i), mybir.AxisListType.X, ALU.min).then_inc(s_range, 1)
                v.tensor_reduce(step[:, b:b + 1], score_of(i), mybir.AxisListType.X, ALU.max).then_inc(s_range, 1)

            def find_threshold():
                dve.wait_ge(s_range, 2 * NI)
                link(v.tensor_tensor(step, step, lo, ALU.subtract))
                link(v.tensor_scalar(step, step, 0.5, None, ALU.mult))
                link(v.memset(hi, -TAKEN))
                dve.wait_ge(s_caus, NI)
                with dve.Fori(0, HALVINGS):
                    v.tensor_tensor(cand, lo, step, ALU.add).then_inc(s_halve, 1)
                    dve.wait_ge(s_halve, 1)
                    for b, i in enumerate(IDX_BLOCKS):
                        if b:
                            dve.wait_ge(s_halve, b + 1)
                        v.tensor_scalar(above[:, 0:(i + 1) * P], score_of(i), cand[:, b:b + 1], None, ALU.is_ge, ALU.add,
                                        accum_out=count[:, b:b + 1]).then_inc(s_halve, 1)
                    dve.wait_ge(s_halve, NI + 1)
                    v.tensor_scalar(good, count, float(TOPK), None, ALU.is_ge).then_inc(s_halve, 1)
                    dve.wait_ge(s_halve, NI + 2)
                    v.tensor_tensor(count, good, step, ALU.mult).then_inc(s_halve, 1)
                    v.scalar_tensor_tensor(good, good, -TAKEN, cand, ALU.mult, ALU.add).then_inc(s_halve, 1)
                    dve.wait_ge(s_halve, NI + 4)
                    v.tensor_tensor(lo, lo, count, ALU.add).then_inc(s_halve, 1)
                    v.tensor_tensor(hi, hi, good, ALU.min).then_inc(s_halve, 1)
                    v.tensor_scalar(step, step, 0.5, None, ALU.mult).then_inc(s_halve, 1)
                    dve.wait_ge(s_halve, NI + 7)
                    dve.sem_clear(s_halve)

            def take_above():
                for b, i in enumerate(IDX_BLOCKS):
                    n = (i + 1) * P
                    if b:
                        dve.wait_ge(s_count, 2 * b)
                    v.tensor_scalar(above[:, 0:n], score_of(i), hi[:, b:b + 1], None, ALU.is_ge, ALU.add,
                                    accum_out=count[:, b:b + 1]).then_inc(s_count, 1)
                    dve.wait_ge(s_count, 2 * b + 1)
                    v.scalar_tensor_tensor(score_of(i), above[:, 0:n], TAKEN, score_of(i), ALU.mult, ALU.add).then_inc(s_count, 1)
                dve.wait_ge(s_count, 2 * NI)
                v.tensor_scalar(need, count, -1.0, float(TOPK), ALU.mult, ALU.add).then_inc(s_need, 1)
                dve.wait_ge(s_most, 1)
                link(v.tensor_scalar(most, most, 1.0 / ROUND, 0.5 - 0.5 / ROUND, ALU.mult, ALU.add))
                link(v.tensor_scalar(most, most, MAGIC, None, ALU.add))
                link(v.tensor_scalar(most, most, MAGIC, None, ALU.subtract))
                link(v.tensor_copy(rounds[:], most))

            def top_keys(i):
                sc = score_of(i)
                b = i - IDX_BLOCKS[0]
                mine = need[:, b:b + 1]
                with dve.Fori(0, dve.value_load(rounds[0:1, b:b + 1], min_val=1, max_val=TOPK // ROUND)):
                    v.max(m8[:], sc).then_inc(s_round, 1)
                    v.tensor_scalar(limit, ramp, mine, 2.0, ALU.is_lt, ALU.mult).then_inc(s_round, 1)
                    dve.wait_ge(s_round, 2)
                    v.tensor_scalar(limit, limit, 1.0, -TAKEN, ALU.subtract, ALU.mult).then_inc(s_round, 1)
                    v.tensor_scalar(mine, mine, float(ROUND), None, ALU.subtract).then_inc(s_round, 1)
                    dve.wait_ge(s_round, 4)
                    v.tensor_tensor(m8[:], m8[:], limit, ALU.min).then_inc(s_round, 1)
                    dve.wait_ge(s_round, 5)
                    v.match_replace(sc, m8[:], sc, TAKEN).then_inc(s_round, 1)
                    dve.wait_ge(s_round, 6)
                    dve.sem_clear(s_round)
                v.tensor_scalar(bias_of(i), sc, TAKEN, -BIG, ALU.not_equal, ALU.mult).then_inc(s_mask, 1)

            rotate(3, P, 48 + 96)
            dve.wait_ge(s_ones, 1 + ROUND)
            find_threshold()
            take_above()
            for i in IDX_BLOCKS:
                top_keys(i)
            dve.wait_ge(s_mask, len(IDX_BLOCKS))
            dve.wait_ge(s_vones, 5)

            def row_max(h, x):
                i = NB - 1 - x
                u = NB * h + x
                dve.wait_ge(s_lg, u + 1)
                if u == NB * h:
                    if h >= 1:
                        dve.wait_ge(s_mp, h)
                src = two(2 * (u % 2))[:, 0:(i + 1) * P]
                v.tensor_tensor_reduce(src, src, bias_of(i), 1.0, -3.0e38, ALU.add, ALU.max, mx[:, i:i + 1]).then_inc(s_mx, 1)

            def max_parts(h):
                dve.wait_ge(s_mx, NB * (h + 1))
                if h >= 1:
                    dve.wait_ge(s_mt, h)
                link(v.tensor_scalar(mparts[:, 0:NB], mx[:], -1.0, None, ALU.mult))
                v.scalar_tensor_tensor(mparts[:, NB:2 * NB], mx[:], -1.0, mparts[:, 0:NB], ALU.mult, ALU.subtract).then_inc(s_mp, 1)

            def max_rows(h):
                dve.wait_ge(s_mt, h + 1)
                if h == 0:
                    dve.wait_ge(s_delta, 16)
                if h >= 2:
                    dve.wait_ge(s_st, PV_AT[(h - 2, 1, NB - 1)] + 1)
                src = ps[0:16, 4 + ST_AT[(h, -1, 0)] % 2, :].bitcast(BF16)[:, 0:P]
                v.tensor_tensor(mrow[h % 2][:], src.rearrange("p (o n) -> p o n", o=1).broadcast_to([16, NB, P]), delta[:],
                                ALU.mult).then_inc(s_mrow, 1)

            def head_out(h, sb):
                dve.wait_ge(s_pv, PV_AT[(h, sb, 4 * sb + 3)] + 1)
                r, d = rows(h), rows(h + 1)
                if 2 * h + sb:
                    dve.wait_ge(s_o, 2 * h + sb)
                link(v.reciprocal(rden[r, :], ps[d, 6 + sb, :]))
                v.tensor_tensor(ya[r, h // 2, HALF * sb:HALF * sb + HALF], ps[r, 6 + sb, :], rden[r, :], ALU.mult).then_inc(s_o, 1)

            def gate_sum(kt):
                dve.wait_ge(s_gw[kt % 2], 16 * (kt // 2 + 1))
                if kt == 0:
                    v.tensor_scalar(gate[:], gw[:, 0, :], csilu[:, 0:1], None, ALU.mult).then_inc(s_gacc, 1)
                else:
                    dve.wait_ge(s_gacc, kt)
                    v.scalar_tensor_tensor(gate[:], gw[:, kt % 2, :], csilu[:, kt:kt + 1], gate[:], ALU.mult, ALU.add).then_inc(s_gacc, 1)

            def pair_gate(t):
                dve.wait_ge(s_yn, t + 1)
                v.scalar_tensor_tensor(ya[:, t, :], ya[:, t, :], vec[:, V_GA + t:V_GA + t + 1], azs[:, t, :],
                                       ALU.mult, ALU.mult).then_inc(s_ya, 1)

            def low_y(b, part):
                dve.wait_ge(s_yH, Y_AT[(b, part)] + 1)
                k = slice(NT * part, NT * part + NT)
                v.tensor_tensor(yL[b % 2][:, k, :], (yconv, ya)[part][:, :, P * b:P * b + P],
                                yH[b % 2][:, k, :].bitcast(F32), ALU.subtract).then_inc(s_yL, 1)

            for x in range(NB):
                row_max(0, x)
            max_parts(0)
            max_rows(0)
            for h in range(NH):
                more = h + 1 < NH
                for x in range(NB - 1):
                    if x == 4 and h:
                        head_out(h - 1, 1)
                    if more:
                        row_max(h + 1, x)
                head_out(h, 0)
                if more:
                    row_max(h + 1, NB - 1)
                    max_parts(h + 1)
                    max_rows(h + 1)
                if 2 <= h <= 5:
                    gate_sum(2 * h - 4)
                    gate_sum(2 * h - 3)
                if h in (3, 5, 7):
                    pair_gate(h // 2 - 1)
            low_y(0, 0)
            low_y(1, 0)
            dve.wait_ge(s_gp, 1)
            dve.wait_ge(s_bg, 16)
            v.tensor_tensor(gate[:], two(2), bgate[:], ALU.add).then_inc(s_gate, 1)
            head_out(NH - 1, 1)
            pair_gate(NT - 1)
            low_y(0, 1)
            low_y(1, 1)
            dve.wait_ge(s_gate, 1)
            dve.wait_ge(s_nf, 16)
            for b in range(NB):
                dve.wait_ge(s_op, b + 1)
                if b >= 2:
                    dve.wait_ge(s_fin, b - 1)
                v.tensor_tensor(te[:, b % 2, :], two(2 * (b % 2)), gate[:], ALU.mult).then_inc(s_og, 1)
                dve.wait_ge(s_og, b + 1)
                dve.wait_ge(s_xe[b % 2], 16 * (b // 2 + 1))
                v.tensor_tensor(te[:, b % 2, :], te[:, b % 2, :], xe[:, b % 2, :], ALU.add).then_inc(s_res, 1)
                if b + 2 < NB:
                    low_y(b + 2, 0)
                    low_y(b + 2, 1)
                dve.wait_ge(s_fsq, b + 1)
                v.tensor_scalar(fin[:, b:b + 1], fin[:, b:b + 1], 1.0 / D, EPS, ALU.mult, ALU.add).then_inc(s_fv, 1)
                dve.wait_ge(s_fs, b + 1)
                link(v.reciprocal(finr[:, b:b + 1], finr[:, b:b + 1]))
                if b >= 2:
                    dve.wait_ge(s_out[b % 2], 16 * (b // 2))
                v.scalar_tensor_tensor(oe[:, b % 2, :], te[:, b % 2, :], finr[:, b:b + 1], normf[:], ALU.mult, ALU.mult).then_inc(s_fin, 1)

        @block.gpsimd
        def _(pool):
            g = nc.gpsimd
            g.memset(onesB[:], 1.0).then_inc(s_vones, 1)

            def split_low(n):
                m = 72 if n == 0 else P
                pool.wait_ge(s_wH, n + 1)
                g.tensor_tensor(wL[:, n % 2, :, 0:m], raw[:, n % NRAW, :, 0:m], wH[:, n % 2, :, 0:m].bitcast(F32),
                                ALU.subtract).then_inc(s_wL, 1)

            split_low(0)
            split_low(1)
            for kt in HL_POOL:
                low_h(g, pool, kt, s_hLp)
            for kind, n in SCHEDULE:
                if kind == "unit":
                    sec, t = UNITS[n]
                    if sec != "cb" and n + 2 < NU and n != EARLY:
                        split_low(n + 2)
                    if sec == "cb":
                        pool.wait_ge(s_evac, UNIT[("cu", t)] + 1)
                        if t == 0:
                            pool.wait_ge(s_splL, 3 * NT)
                            g.memset(convs[:, 0:2], 0.0).then_inc(s_pad, 1)
                        g.tensor_tensor(convs[:, 2:2 + S], convc[:], convu[:], ALU.mult).then_inc(s_cvs, 1)
                        split_low(n + 2)
                        pool.wait_ge(s_cvt, 3 * t + 2)
                        g.tensor_tensor(conv0[:], conv0[:], conv1[:], ALU.add).then_inc(s_cvy, 1)
                        pool.wait_ge(s_cvt, 3 * t + 3)
                        pool.wait_ge(s_cvy, 2 * t + 1)
                        g.tensor_tensor(conv0[:], conv0[:], conv1[:], ALU.add).then_inc(own_pool, 1)
                        pool.wait_ge(own_pool, 3 * t + 1)
                        pool.wait_ge(s_evac, n + 1)
                        g.tensor_tensor(convb[:], convb[:], conv0[:], ALU.mult).then_inc(s_cvy, 1)
                elif kind == "idx":
                    pool.wait_ge(s_score, NIH * (n - 1))
                    pool.wait_ge(s_range, 2 * (n - 1))
                    d = score_of(n)[:, P * n:P * n + P]
                    g.affine_select(out=d, in_=d, compare_op=ALU.is_ge, fill=FUTURE, base=0, pattern=[[-1, P]],
                                    channel_multiplier=1).then_inc(s_caus, 1)
                    if n == 5:
                        split_low(EARLY + 2)
                elif kind == "cn":
                    pool.wait_ge(s_cvr, n + 1)
                    pool.wait_ge(s_cvy, 2 * n + 2)
                    g.tensor_tensor(convb[:], convb[:], conv1[:], ALU.mult).then_inc(own_pool, 1)
                    pool.wait_ge(own_pool, 3 * n + 2)
                    g.tensor_scalar(convb[:], convb[:], vec[:, V_GC + n:V_GC + n + 1], None, ALU.mult).then_inc(own_pool, 1)
                    pool.wait_ge(own_pool, 3 * n + 3)
                    pool.wait_ge(s_evac, UNIT[("cz", n)] + 1)
                    g.tensor_tensor(yconv[:, n, :], yconv[:, n, :], convb[:], ALU.mult).then_inc(s_cvn, 1)
                if (kind, n) == ("unit", 5):
                    g.memset(bias[:, 0:3 * P], 0.0).then_inc(s_vones, 1)
                    pool.wait_ge(s_vones, 2)
                    for i in range(2):
                        d = bias_of(i)[:, P * i:P * i + P]
                        g.affine_select(out=d, in_=d, compare_op=ALU.is_ge, fill=-BIG, base=0, pattern=[[-1, P]],
                                        channel_multiplier=1).then_inc(s_vones, 1)
                if (kind, n) == ("unit", UNIT[("cb", 1)]):
                    pool.wait_ge(s_need, 1)
                    g.partition_all_reduce(most, need, P, bass.bass_isa.ReduceOp.max).then_inc(s_most, 1)
                if (kind, n) == ("unit", UNIT[("av", 0)]):
                    pool.wait_ge(s_idx, NIH * len(IDX_BLOCKS))
                    g.memset(V[:, :, :, HD:2 * HD], 1.0).then_inc(s_vones, 1)
                if SPLITS.get((kind, n)) == "ak":
                    for t in range(NT):
                        section_low(g, pool, SPLITS[(kind, n)], t)
            def pair_square(t):
                pool.wait_ge(s_o, 4 * (t + 1))
                if t == 0:
                    g.memset(onesq[:], 1.0).then_inc(s_onesq, 1)
                else:
                    pool.wait_ge(s_yn, t)
                g.tensor_tensor(ysq[:], ya[:, t, :], ya[:, t, :], ALU.mult).then_inc(s_ysq, 1)

            def pair_scale(t):
                pool.wait_ge(s_yrs, 2 * t + 2)
                g.tensor_tensor(ya[:, t, :], ya[:, t, :], ysq[:], ALU.mult).then_inc(s_yn, 1)

            def out_low(h):
                for ct in OUT_TILES[h]:
                    done = sum(len(OUT_TILES[x]) for x in range(1, h)) + OUT_TILES[h].index(ct)
                    pool.wait_ge(s_woH, done + 1)
                    g.tensor_tensor(hL[:, ct, :], wo[:, ct, :], hH[:, ct, :].bitcast(F32),
                                    ALU.subtract).then_inc(s_woL, 1)

            out_low(1)
            for t in range(NT):
                pair_square(t)
                if t < NT - 1:
                    out_low(2 * t + 2)
                pair_scale(t)
                if t < NT - 1:
                    out_low(2 * t + 3)


INPUTS = ("x", "positions", "w_ada", "w_out", "norm_f", "b_gate", "w_ik", "w_units", "vecs", "ident_f", "ident_b",
          "pairs", "delta")


def kernel(x, c, positions, w_ada, b_ada, norm_in, w_in, conv_w, conv_b, gn_conv, gn_attn, w_out, norm_f):
    import ml_dtypes
    import concourse.bacc as bacc
    from concourse.bass_utils import run_bass_kernel_spmd

    def columns(v):
        return np.asarray(v).reshape(-1, P).T

    w_in = np.asarray(w_in)
    tiles = np.stack([w_in[:, STARTS[s] + P * t:STARTS[s] + P * t + P] for s, t in UNITS[1:]])
    freq = np.float32(500000.0) ** (-np.arange(ROPE // 2, dtype=np.float32) / np.float32(ROPE // 2))
    row = np.arange(P) % ROPE
    vecs = np.zeros((P, V_COLS), np.float32)
    for at, v in ((V_C, c), (V_NORM, norm_in), (V_BSH, b_ada[:D]), (V_BSC, b_ada[D:2 * D]), (V_CW, conv_w),
                  (V_CB, conv_b), (V_GC, gn_conv), (V_GA, gn_attn)):
        v = columns(v)
        vecs[:, at:at + v.shape[1]] = v
    vecs[:, V_FREQ] = freq[row % (ROPE // 2)]
    vecs[:, V_SIGN] = np.where(row < ROPE // 2, -1.0, 1.0)
    vecs[:, V_EPS] = EPS
    group = np.arange(P) // HD
    arrays = {
        "x": x, "positions": positions, "w_ada": w_ada, "w_out": w_out, "norm_f": norm_f, "b_gate": b_ada[2 * D:],
        "w_ik": w_in[:, 4608:4680].reshape(KT, P, 72).transpose(1, 0, 2),
        "w_units": tiles.reshape(NU - 1, KT, P, P).transpose(0, 2, 1, 3),
        "vecs": vecs, "ident_f": np.eye(P, dtype=np.float32), "ident_b": np.eye(P).astype(ml_dtypes.bfloat16),
        "pairs": (group[:, None] == group[None, :]).astype(np.float32),
        "delta": (np.arange(16)[:, None, None] % NB == np.arange(NB)[None, :, None]).repeat(P, 2).astype(ml_dtypes.bfloat16),
    }
    arrays = {"in_" + k: np.ascontiguousarray(arrays[k]) for k in INPUTS}
    nc = bacc.Bacc("TRN2", target_bir_lowering=False, num_devices=1)
    aps = {k: nc.dram_tensor("in_" + k, arrays["in_" + k].shape, mybir.dt.from_np(arrays["in_" + k].dtype),
                             kind="ExternalInput").ap() for k in INPUTS}
    aps["out"] = nc.dram_tensor("out", (1, S, D), F32, kind="ExternalOutput").ap()
    build(nc, aps)
    return run_bass_kernel_spmd(nc, [arrays], core_ids=[0]).results[0]["out"]
```
